# Optimizing a Trainium2 kernel written in Bass

```python
import jax
import jax.numpy as jnp
from jax import lax
import numpy as np

D_MODEL = 1024
BATCH = 1
SEQ = 1024
DEPTH = 2
DEC_BATCH = 1
DEC_SEQ = 64
PAST_LEN = 128

CHUNK = 64
HEAD_DIM = 64
A_WIDTH = D_MODEL // 4
A_HEADS = A_WIDTH // HEAD_DIM
A_BLOCK = 128
B_WIDTH = D_MODEL // 2
B_HEADS = B_WIDTH // HEAD_DIM
B_KV_HEADS = 2
B_GROUP = B_HEADS // B_KV_HEADS
WINDOW = 128
WIN_CHUNKS = WINDOW // CHUNK
ROT_DIM = HEAD_DIM // 4
ROPE_THETA = 500000.0
ATTN_SCALE = HEAD_DIM ** -0.5
C_WIDTH = D_MODEL // 4
C_HEADS = C_WIDTH // HEAD_DIM
MIX_WIDTH = A_WIDTH + B_WIDTH + C_WIDTH
D_FF = ((8 * D_MODEL // 3 + 255) // 256) * 256
CONV_W = 3
RMS_EPS = 1e-6

OFF_A_U = 0
OFF_A_V = OFF_A_U + A_WIDTH
OFF_B_Q = OFF_A_V + A_WIDTH
OFF_B_K = OFF_B_Q + B_HEADS * HEAD_DIM
OFF_B_V = OFF_B_K + B_KV_HEADS * HEAD_DIM
OFF_C_Q = OFF_B_V + B_KV_HEADS * HEAD_DIM
OFF_C_K = OFF_C_Q + C_WIDTH
OFF_C_V = OFF_C_K + C_WIDTH
OFF_C_O = OFF_C_V + C_WIDTH
OFF_C_G = OFF_C_O + C_WIDTH
IN_WIDTH = OFF_C_G + 2 * C_HEADS

kernel_name = 'hybrid_streaming_encoder_step'

def rmsnorm(x, g):
    xf = x.astype(jnp.float32)
    xf = xf * lax.rsqrt(jnp.mean(xf * xf, axis=-1, keepdims=True) + RMS_EPS)
    return xf.astype(x.dtype) * g

def partial_rotary(x, pos):
    half = ROT_DIM // 2
    inv_freq = ROPE_THETA ** (-jnp.arange(half, dtype=jnp.float32) / half)
    ang = pos.astype(jnp.float32)[:, None] * inv_freq[None, :]
    cos = jnp.cos(ang)[:, None, :]
    sin = jnp.sin(ang)[:, None, :]
    x1 = x[..., :half].astype(jnp.float32)
    x2 = x[..., half:ROT_DIM].astype(jnp.float32)
    rot = jnp.concatenate([x1 * cos - x2 * sin, x2 * cos + x1 * sin], axis=-1).astype(x.dtype)
    return jnp.concatenate([rot, x[..., ROT_DIM:]], axis=-1)

def project(x, pos, norm_g, w_in, gmlp_norm_g, gate_b):
    B_, T, _ = x.shape
    z = rmsnorm(x, norm_g) @ w_in

    def heads(off, n):
        return z[..., off:off + n * HEAD_DIM].reshape(B_, T, n, HEAD_DIM)

    a_u = jax.nn.gelu(heads(OFF_A_U, A_HEADS), approximate=False)
    a_v = rmsnorm(jax.nn.gelu(z[..., OFF_A_V:OFF_A_V + A_WIDTH], approximate=False), gmlp_norm_g)
    a_v = a_v.reshape(B_, T, A_HEADS, HEAD_DIM)
    b_q = partial_rotary(heads(OFF_B_Q, B_HEADS), pos)
    b_k = partial_rotary(heads(OFF_B_K, B_KV_HEADS), pos)
    b_v = heads(OFF_B_V, B_KV_HEADS)
    c_q = heads(OFF_C_Q, C_HEADS)
    c_k = heads(OFF_C_K, C_HEADS) * ATTN_SCALE
    c_v = heads(OFF_C_V, C_HEADS)
    c_o = jax.nn.sigmoid(z[..., OFF_C_O:OFF_C_O + C_WIDTH])
    gates = z[..., OFF_C_G:OFF_C_G + 2 * C_HEADS].astype(jnp.float32) + gate_b.astype(jnp.float32)
    c_logi = gates[..., :C_HEADS]
    c_logf = jax.nn.log_sigmoid(gates[..., C_HEADS:])
    return a_u, a_v, b_q, b_k, b_v, c_q, c_k, c_v, c_o, c_logi, c_logf

def gmlp_mask():
    i = jnp.arange(A_BLOCK)
    return (i[None, :] // CHUNK) <= (i[:, None] // CHUNK)

def gmlp_prompt(u, v, w_s, b_s):
    B_, S = v.shape[:2]
    w = jnp.where(gmlp_mask()[None], w_s, 0.0)
    vb = v.reshape(B_, S // A_BLOCK, A_BLOCK, A_HEADS, HEAD_DIM)
    mixed = jnp.einsum('hij,bgjhd->bgihd', w, vb) + b_s.T[:, :, None]
    return u * mixed.reshape(B_, S, A_HEADS, HEAD_DIM)

def gmlp_sample(u, v, w_s, b_s):
    T = v.shape[1]
    w = jnp.where(gmlp_mask()[None], w_s, 0.0)[:, :T, :T]
    mixed = jnp.einsum('hij,bjhd->bihd', w, v) + b_s[:, :T].T[:, :, None]
    return u * mixed

def sink_softmax(s, sinks):
    sk = jnp.broadcast_to(sinks.reshape(B_KV_HEADS, B_GROUP, 1, 1).astype(jnp.float32), s.shape[:-1] + (1,))
    p = jax.nn.softmax(jnp.concatenate([s, sk], axis=-1), axis=-1)
    return p[..., :-1]

def swa_prompt(q, k, v, sinks):
    B_, S = q.shape[:2]
    nC = S // CHUNK
    qc = q.reshape(B_, nC, CHUNK, B_KV_HEADS, B_GROUP, HEAD_DIM)
    pad = ((0, 0), (WIN_CHUNKS * CHUNK, 0), (0, 0), (0, 0))
    kp = jnp.pad(k, pad).reshape(B_, nC + WIN_CHUNKS, CHUNK, B_KV_HEADS, HEAD_DIM)
    vp = jnp.pad(v, pad).reshape(B_, nC + WIN_CHUNKS, CHUNK, B_KV_HEADS, HEAD_DIM)
    kb = jnp.concatenate([kp[:, j:j + nC] for j in range(WIN_CHUNKS + 1)], axis=2)
    vb = jnp.concatenate([vp[:, j:j + nC] for j in range(WIN_CHUNKS + 1)], axis=2)
    s = jnp.einsum('bcqkgd,bcskd->bckgqs', qc, kb).astype(jnp.float32) * ATTN_SCALE
    key_pos = (jnp.arange(nC)[:, None] - WIN_CHUNKS) * CHUNK + jnp.arange((WIN_CHUNKS + 1) * CHUNK)[None, :]
    s = jnp.where((key_pos >= 0)[None, :, None, None, None, :], s, -jnp.inf)
    p = sink_softmax(s, sinks)
    o = jnp.einsum('bckgqs,bcskd->bcqkgd', p.astype(vb.dtype), vb)
    return o.reshape(B_, S, B_WIDTH)

def swa_sample(q, k_new, v_new, win_k, win_v, sinks):
    B_, T = q.shape[:2]
    kk = jnp.concatenate([win_k.astype(k_new.dtype), k_new], axis=1)
    vv = jnp.concatenate([win_v.astype(v_new.dtype), v_new], axis=1)
    qg = q.reshape(B_, T, B_KV_HEADS, B_GROUP, HEAD_DIM)
    s = jnp.einsum('bqkgd,bskd->bkgqs', qg, kk).astype(jnp.float32) * ATTN_SCALE
    p = sink_softmax(s, sinks)
    o = jnp.einsum('bkgqs,bskd->bqkgd', p.astype(vv.dtype), vv)
    return o.reshape(B_, T, B_WIDTH)

def mlstm_chunk(carry, inp):
    C, n, m = carry
    q, k, v, logi, logf = inp
    L = q.shape[2]
    b = jnp.cumsum(logf, axis=-1)
    causal = jnp.tril(jnp.ones((L, L), dtype=bool))
    D = jnp.where(causal, b[..., :, None] - b[..., None, :] + logi[..., None, :], -jnp.inf)
    inter = b + m[..., None]
    m_t = jnp.maximum(inter, jnp.max(D, axis=-1))
    w_inter = jnp.exp(inter - m_t)
    S = jnp.einsum('bhtd,bhsd->bhts', q, k) * jnp.exp(D - m_t[..., None])
    num = w_inter[..., None] * jnp.einsum('bhvk,bhtk->bhtv', C, q) + jnp.einsum('bhts,bhsv->bhtv', S, v)
    den = w_inter * jnp.einsum('bhk,bhtk->bht', n, q) + jnp.sum(S, axis=-1)
    h = num / jnp.maximum(jnp.abs(den), jnp.exp(-m_t))[..., None]
    m_new = m_t[..., -1]
    decay = jnp.exp(b[..., -1] + m - m_new)
    w_s = jnp.exp(b[..., -1:] - b + logi - m_new[..., None])
    C_new = decay[..., None, None] * C + jnp.einsum('bhs,bhsv,bhsk->bhvk', w_s, v, k)
    n_new = decay[..., None] * n + jnp.einsum('bhs,bhsk->bhk', w_s, k)
    return (C_new, n_new, m_new), h

def mlstm(q, k, v, logi, logf, carry, chunk):
    B_, T, H, D = q.shape
    nC = T // chunk

    def blocks(a):
        a = a.astype(jnp.float32).reshape((B_, nC, chunk) + a.shape[2:])
        return jnp.moveaxis(a, (1, 3), (0, 2))

    carry = (carry[0].astype(jnp.float32), carry[1].astype(jnp.float32), carry[2].astype(jnp.float32))
    carry, h = lax.scan(mlstm_chunk, carry, (blocks(q), blocks(k), blocks(v), blocks(logi), blocks(logf)))
    h = jnp.transpose(h, (1, 0, 3, 2, 4)).reshape(B_, T, H * D)
    return h, carry

def conv_ffn(x, g, w_up, conv_w, conv_b, w_down, conv_buf):
    up = rmsnorm(x, g) @ w_up
    T = up.shape[1]
    full = jnp.concatenate([conv_buf.astype(up.dtype), up], axis=1)
    c = conv_b + full[:, 0:T] * conv_w[0]
    for j in range(1, CONV_W):
        c = c + full[:, j:j + T] * conv_w[j]
    y = (jax.nn.gelu(c[..., :D_FF], approximate=False) * c[..., D_FF:]) @ w_down
    return y, full[:, -(CONV_W - 1):]

def layer(x, pos, lp, cache):
    B_, T, _ = x.shape
    a_u, a_v, b_q, b_k, b_v, c_q, c_k, c_v, c_o, c_logi, c_logf = project(
        x, pos, lp['attn_norm'], lp['w_in'], lp['gmlp_norm'], lp['mlstm_gate_b'])
    if cache is None:
        a_out = gmlp_prompt(a_u, a_v, lp['gmlp_w'], lp['gmlp_b'])
        b_out = swa_prompt(b_q, b_k, b_v, lp['attn_sinks'])
        carry0 = (jnp.zeros((B_, C_HEADS, HEAD_DIM, HEAD_DIM), jnp.float32),
                  jnp.zeros((B_, C_HEADS, HEAD_DIM), jnp.float32),
                  jnp.zeros((B_, C_HEADS), jnp.float32))
        c_h, (C, n, m) = mlstm(c_q, c_k, c_v, c_logi, c_logf, carry0, CHUNK)
        conv_buf = jnp.zeros((B_, CONV_W - 1, 2 * D_FF), x.dtype)
    else:
        win_k, win_v, C0, n0, m0, conv_buf = cache
        a_out = gmlp_sample(a_u, a_v, lp['gmlp_w'], lp['gmlp_b'])
        b_out = swa_sample(b_q, b_k, b_v, win_k, win_v, lp['attn_sinks'])
        c_h, (C, n, m) = mlstm(c_q, c_k, c_v, c_logi, c_logf, (C0, n0, m0), T)
    mixed = jnp.concatenate([a_out.reshape(B_, T, A_WIDTH), b_out, (c_o * c_h).astype(x.dtype)], axis=-1)
    x = x + mixed @ lp['w_out']
    y, conv_state = conv_ffn(x, lp['ffn_norm'], lp['w_up'], lp['conv_w'], lp['conv_b'], lp['w_down'], conv_buf)
    x = x + y
    if cache is None:
        return x, (b_k[:, -WINDOW:], b_v[:, -WINDOW:], C, n, m, conv_state)
    return x, (a_v.reshape(B_, T, A_WIDTH), b_k, b_v, C, n, m, conv_state)

def setup_inputs(seed: int = 0) -> dict:
    key = jax.random.key(seed)
    ks = jax.random.split(key, 23)

    def nrm(k, shape, scale):
        return scale * jax.random.normal(k, shape, jnp.float32)

    return {
        'x_prompt': nrm(ks[0], (BATCH, SEQ, D_MODEL), 1.0),
        'x_sample': nrm(ks[1], (DEC_BATCH, DEC_SEQ, D_MODEL), 1.0),
        'cache_k': nrm(ks[2], (DEPTH, DEC_BATCH, WINDOW, B_KV_HEADS, HEAD_DIM), 1.0),
        'cache_v': nrm(ks[3], (DEPTH, DEC_BATCH, WINDOW, B_KV_HEADS, HEAD_DIM), 1.0),
        'state_C': nrm(ks[4], (DEPTH, DEC_BATCH, C_HEADS, HEAD_DIM, HEAD_DIM), 0.1),
        'state_n': nrm(ks[5], (DEPTH, DEC_BATCH, C_HEADS, HEAD_DIM), 0.1),
        'state_m': nrm(ks[6], (DEPTH, DEC_BATCH, C_HEADS), 1.0),
        'cache_conv': nrm(ks[7], (DEPTH, DEC_BATCH, CONV_W - 1, 2 * D_FF), 1.0),
        'attn_norm': 1.0 + nrm(ks[8], (DEPTH, D_MODEL), 0.02),
        'w_in': nrm(ks[9], (DEPTH, D_MODEL, IN_WIDTH), D_MODEL ** -0.5),
        'gmlp_norm': 1.0 + nrm(ks[10], (DEPTH, A_WIDTH), 0.02),
        'gmlp_w': nrm(ks[11], (DEPTH, A_HEADS, A_BLOCK, A_BLOCK), A_BLOCK ** -0.5),
        'gmlp_b': 1.0 + nrm(ks[12], (DEPTH, A_HEADS, A_BLOCK), 0.02),
        'attn_sinks': nrm(ks[13], (DEPTH, B_HEADS), 0.5),
        'mlstm_gate_b': jnp.concatenate([nrm(ks[14], (DEPTH, C_HEADS), 0.1),
                                         3.0 + nrm(ks[15], (DEPTH, C_HEADS), 0.5)], axis=-1),
        'w_out': nrm(ks[16], (DEPTH, MIX_WIDTH, D_MODEL), MIX_WIDTH ** -0.5),
        'ffn_norm': 1.0 + nrm(ks[17], (DEPTH, D_MODEL), 0.02),
        'w_up': nrm(ks[18], (DEPTH, D_MODEL, 2 * D_FF), D_MODEL ** -0.5),
        'conv_w': nrm(ks[19], (DEPTH, CONV_W, 2 * D_FF), CONV_W ** -0.5),
        'conv_b': nrm(ks[20], (DEPTH, 2 * D_FF), 0.02),
        'w_down': nrm(ks[21], (DEPTH, D_FF, D_MODEL), D_FF ** -0.5),
        'final_norm': 1.0 + nrm(ks[22], (D_MODEL,), 0.02),
    }

def reference(x_prompt, x_sample, cache_k, cache_v, state_C, state_n, state_m, cache_conv,
              attn_norm, w_in, gmlp_norm, gmlp_w, gmlp_b, attn_sinks, mlstm_gate_b, w_out,
              ffn_norm, w_up, conv_w, conv_b, w_down, final_norm):
    pos_prompt = jnp.arange(x_prompt.shape[1], dtype=jnp.int32)
    pos_sample = PAST_LEN + jnp.arange(x_sample.shape[1], dtype=jnp.int32)
    xp, xs = x_prompt, x_sample
    p_st, s_st = [], []
    for l in range(DEPTH):
        lp = {'attn_norm': attn_norm[l], 'w_in': w_in[l], 'gmlp_norm': gmlp_norm[l], 'gmlp_w': gmlp_w[l],
              'gmlp_b': gmlp_b[l], 'attn_sinks': attn_sinks[l], 'mlstm_gate_b': mlstm_gate_b[l],
              'w_out': w_out[l], 'ffn_norm': ffn_norm[l], 'w_up': w_up[l], 'conv_w': conv_w[l],
              'conv_b': conv_b[l], 'w_down': w_down[l]}
        xp, st = layer(xp, pos_prompt, lp, None)
        p_st.append(st)
        xs, st = layer(xs, pos_sample, lp,
                       (cache_k[l], cache_v[l], state_C[l], state_n[l], state_m[l], cache_conv[l]))
        s_st.append(st)
    y_prompt = rmsnorm(xp, final_norm)
    y_sample = rmsnorm(xs, final_norm)

    def stk(states, i):
        return jnp.stack([s[i] for s in states], axis=0)

    return (y_prompt, y_sample,
            stk(p_st, 0), stk(p_st, 1), stk(p_st, 2), stk(p_st, 3), stk(p_st, 4), stk(p_st, 5),
            stk(s_st, 0), stk(s_st, 1), stk(s_st, 2), stk(s_st, 3), stk(s_st, 4), stk(s_st, 5), stk(s_st, 6))


_drawn_inputs = setup_inputs


def setup_inputs(seed=0):
    import zlib

    import numpy as np

    out = dict(_drawn_inputs(seed))
    spreads = {}
    factors = {'gmlp_norm': 2.703, 'gmlp_b': 3.349, 'attn_sinks': 8.0, 'final_norm': 2.808}
    for name, (base, spread) in spreads.items():
        noise = np.random.default_rng([zlib.crc32(name.encode()), seed]).standard_normal(out[name].shape)
        drawn = base * np.exp(spread * noise) if base else spread * noise
        out[name] = jnp.asarray(drawn.astype(out[name].dtype))
    for name, factor in factors.items():
        out[name] = (out[name] * factor).astype(out[name].dtype)
    return out
```

```python
from contextlib import ExitStack

import numpy as np

import concourse.bass as bass
from concourse import mybir

F32 = mybir.dt.float32
F32R = mybir.dt.float32r
ALU = mybir.AluOpType
ACT = mybir.ActivationFunctionType
AX = mybir.AxisListType
ds = bass.ds

P = 128
D = 1024
KT = D // P
SEQ = 1024
DEPTH = 2
DEC = 64
PAST = 128
HD = 64
FF = 2816
NF = FF // P
PAD = 2
TC = SEQ + PAD + DEC
SOFF = SEQ + PAD
CH = [(0, 364), (364, 364), (728, 362)]
NB = SEQ // P
TOK = [(i * P, P) for i in range(NB)] + [(SOFF, DEC)]
NTOK = len(TOK)
ZW = 2312
A_U, A_V, B_Q, B_K, B_V, C_Q, C_K, C_V, C_O, C_G = 0, 256, 512, 1024, 1152, 1280, 1536, 1792, 2048, 2304
ZA, ZB = 512, 450
SCALE = HD ** -0.5
EPS = 1e-6
BIG = 1e30
ROT = 16
THETA = 500000.0

CI, CU, CM, CCOS, CSIN = 0, P, 2 * P, 3 * P, 3 * P + NTOK * ROT
CW = 3 * P + 2 * NTOK * ROT


def constants():
    t = np.zeros((P, CW), np.float32)
    t[:, CI:CI + P] = np.eye(P)
    t[:, CU:CU + P] = np.triu(np.ones((P, P)))
    t[:, CM:CM + P] = np.where(np.tril(np.ones((P, P))) > 0, 0.0, -BIG)
    half = ROT // 2
    inv = (np.float32(THETA) ** (-np.arange(half, dtype=np.float32) / np.float32(half))).astype(np.float32)
    for i in range(NTOK):
        pos = (np.arange(P) + (i * P if i < NB else PAST)).astype(np.float32)
        ang = (pos[:, None] * inv[None, :]).astype(np.float32)
        c, s = np.cos(ang), np.sin(ang)
        t[:, CCOS + i * ROT:CCOS + (i + 1) * ROT] = np.concatenate([c, c], 1)
        t[:, CSIN + i * ROT:CSIN + (i + 1) * ROT] = np.concatenate([-s, s], 1)
    return t


def wait(eng, sem, value):
    if isinstance(value, int) and value <= 0:
        return
    eng.wait_ge(sem, value)


def settle(eng, settled):
    eng.sem_inc(settled, 1)


class Chain:

    def __init__(self, eng, sem, base):
        self.eng, self.sem, self.base, self.n = eng, sem, base, 0

    def link(self, ins):
        self.n += 1
        ins.then_inc(self.sem, 1)
        self.eng.wait_ge(self.sem, self.base + self.n)


def build(nc, I, O):
    ctx = ExitStack()

    def sem(name):
        return ctx.enter_context(nc.semaphore(name))

    def sb(name, shape, dt=F32, c=ctx):
        return c.enter_context(nc.sbuf_tensor(name, shape, dt))

    with ctx:
        bank = [ctx.enter_context(nc.psum_tensor(f"bank{i}", [P, 512], F32)) for i in range(8)]
        z_dram = nc.dram_tensor("z_scratch", (NTOK * P, ZW), F32, kind="Internal").ap()

        xT = sb("xT", [P, KT, TC])
        actH = sb("actH", [P, KT, TC], F32R)
        actL = sb("actL", [P, KT, TC], F32R)
        ident = sb("ident", [P, P])
        ones = sb("ones", [P, P])
        gains = sb("gains", [P, (2 * DEPTH + 1) * KT])
        rstd_cu = sb("rstd_cu", [P, 2, TC])
        rstd = rstd_cu[:, 0]
        cu = rstd_cu[:, 1]
        upb = sb("upb", [P, PAD + TC])
        convc = sb("convc", [P, 264])
        convst = sb("convst", [P, 4, 2 * NF])
        stat = sb("stat", [P, 3 * NTOK])
        rt = stat[:, 0:NTOK]
        ms = stat[:, NTOK:2 * NTOK]
        mhalf = stat[:, 2 * NTOK:3 * NTOK]

        with ExitStack() as c:
            grows = sb("grows", [(2 * DEPTH + 1) * KT, P], c=c)
            rawz = sb("rawz", [P, KT, ZA], c=c)
            wzH = [sb("wzH0", [P, KT, ZA], F32R, c=c), sb("wzH1", [P, KT, ZB], F32R, c=c)]
            wzL = [sb("wzL0", [P, KT, ZA], F32R, c=c), sb("wzL1", [P, KT, ZB], F32R, c=c)]
            zst = sb("zst", [P, 3, ZA], c=c)
            identr = sb("identr", [P, P], F32R, c=c)
            xin = yst = rawz[:, 0:4].rearrange("p (b a) n -> p b (a n)", b=2)
        with ExitStack() as c:
            zb = [sb(f"zb{i}", [P, ZW], c=c) for i in range(2)]
            table = sb("table", [P, CW], c=c)
            rows = sb("rows", [88, 3, P], c=c)
            gw = sb("gw", [P, 4, P], c=c)
            gwT = sb("gwT", [P, 4, P], c=c)
            gbias = sb("gbias", [P, 2, P], c=c)
            ggain = sb("ggain", [P, 256], c=c)
            sink = sb("sink", [P, 4], c=c)
            nsink = sb("nsink", [P, 4], c=c)
            gateb = sb("gateb", [P, 8], c=c)
            qp = sb("qp", [P, 512], c=c)
            rp1 = sb("rp1", [P, 10, ROT], c=c)
            rp2 = sb("rp2", [P, 10, ROT], c=c)
            ckin = sb("ckin", [P, P], c=c)
            vprev = sb("vprev", [P, P], c=c)
            kTw = sb("kTw", [P, 2 * P], c=c)
            bqT = sb("bqT", [P, 4, P], c=c)
            prob = [sb(f"prob{i}", [P, 4, 2 * P], c=c) for i in range(2)]
            pT = [sb(f"pT{i}", [P, 2, 4, P], c=c) for i in range(2)]
            mx = sb("mx", [P, 2, 4], c=c)
            nm = sb("nm", [P, 2, 4], c=c)
            es = sb("es", [P, 2, 4], c=c)
            rs = sb("rs", [P, 2, 4], c=c)
            uT = sb("uT", [P, 2, P], c=c)
            vsq = sb("vsq", [P, 256], c=c)
            vss = sb("vss", [P, 1], c=c)
            rv = sb("rv", [P, 1], c=c)
            vn = sb("vn", [P, 256], c=c)
            mixA = sb("mixA", [P, 2, P], c=c)
            qz = sb("qz", [P, 4, P], c=c)
            ckT = sb("ckT", [P, 2, P], c=c)
            g8 = sb("g8", [P, 8], c=c)
            ax = sb("ax", [P, 4], c=c)
            lf = sb("lf", [P, 4], c=c)
            bb = sb("bb", [P, 8], c=c)
            aa = sb("aa", [P, 4], c=c)
            dA = sb("dA", [P, 4 * P], c=c)
            Am = sb("Am", [P, 4, P], c=c)
            cm = sb("cm", [P, 4], c=c)
            G = sb("G", [P, 4], c=c)
            mp = sb("mp", [P, 4], c=c)
            sm = sb("sm", [P, 16], c=c)
            ex = sb("ex", [P, 16], c=c)
            Wt = sb("Wt", [P, 4, P], c=c)
            WTs = sb("WTs", [P, 4, P], c=c)
            Vx = sb("Vx", [P, 4, HD + 1], c=c)
            kw = sb("kw", [P, 256], c=c)
            nd = sb("nd", [P, 4, HD + 1], c=c)
            dn = sb("dn", [P, 4], c=c)
            eo = sb("eo", [P, 256], c=c)
            hc = sb("hc", [P, 256], c=c)
            CN = sb("CN", [P, 2, HD + 1], c=c)
            dec = sb("dec", [P, 2], c=c)
            stin = sb("stin", [HD + 1, 256], c=c)
            stout = sb("stout", [HD + 1, 2, P], c=c)
        with ExitStack() as c:
            wH = sb("wH", [P, 6, KT, P], F32R, c=c)
            wL = sb("wL", [P, 6, KT, P], F32R, c=c)
            raw = sb("raw", [P, 3, KT, P], c=c)
            gHL = sb("gHL", [P, 3, 2, TC], F32R, c=c)
            cv = sb("cv", [P, TC], c=c)
            cvo = cv[0:88, 0:2 * P].rearrange("p (s n) -> p s n", s=2)
        with ExitStack() as c:
            c.enter_context(nc.sbuf_tensor("weights_place", [P, 15 * KT * P * 4], mybir.dt.uint8))
            diag = sb("diag", [P, NTOK, P], c=c)

        settled = sem("settled")
        const_in, s_ones, xin_in0, xin_in1, xin_tp, xin_ea, xin_ev, x_done = map(sem, (
            "const_in", "s_ones", "xin_in0", "xin_in1", "xin_tp", "xin_ea", "xin_ev", "x_done"))
        rows_in, rows_tp, gains_r, conv_r = map(sem, ("rows_in", "rows_tp", "gains_r", "conv_r"))
        sq_r, acc_r, act_h, act_l, ssq_mm, ms_r, rt_r = map(sem, (
            "sq_r", "acc_r", "act_h", "act_l", "ssq_mm", "ms_r", "rt_r"))
        rz_in, wz_h, wz_l, z_mm, z_ev = map(sem, ("rz_in", "wz_h", "wz_l", "z_mm", "z_ev"))
        z_st = [sem(f"z_st{i}") for i in range(3)]
        par_in, z_in0, z_in1, par_tp, gwT_r, ck_r, cn_r, init_r, v_init = map(sem, (
            "par_in", "z_in0", "z_in1", "par_tp", "gwT_r", "ck_r", "cn_r", "init_r", "v_init"))
        z_in = [z_in0, z_in1]
        MIX = ("rope_r qp_r tC_r tU_r tB_r ax_r lg_r lf_r cum_r dA_r A_r A_used sm_r ex_r D_r P_r qk_r W_r WT_r WTs_r "
               "vms_r rv_r vn_r bq_r kT_r cT_r mix_r mA_r int_r num_r t1_r hc_r hT_r eo_r kw_r kwmm_r pv_r "
               "hA_r hB_r hC_r vx_r keep_r blk_done").split()
        S = {n: sem(n) for n in MIX}
        S2 = {n: [sem(f"{n}{i}") for i in range(2)] for n in ("S_r", "nm_r", "e_r", "p_r", "PT_r", "pTa_r", "pTv_r")}
        kv_st, gv_st, sto_r, stt_r, st_st, mix_seq, act_seq = map(sem, (
            "kv_st", "gv_st", "sto_r", "stt_r", "st_st", "mix_seq", "act_seq"))
        raw_in = [sem(f"raw_in{i}") for i in range(3)]
        w_h, w_l, mm, bank_free, w_used, diag_r, rs_mm, rstd_r = map(sem, (
            "w_h", "w_l", "mm", "bank_free", "w_used", "diag_r", "rs_mm", "rstd_r"))
        up_r, c0_r, tap_r, gelu_r, gmul_r, g_h, g_l, cvs_r, cvt_r, cvo_r, cvo_st, up_seq, rp_r = map(sem, (
            "up_r", "c0_r", "tap_r", "gelu_r", "gmul_r", "g_h", "g_l", "cvs_r", "cvt_r", "cvo_r", "cvo_st", "up_seq", "rp_r"))
        y_tp, y_ea, y_ev, y_st0, y_st1, identr_r = map(sem, ("y_tp", "y_ea", "y_ev", "y_st0", "y_st1", "identr_r"))

        N_W = KT + 3 * NF
        N_USE = KT + 2 * NF + KT * (NF // 2)
        NG = NF // 2

        def split3(pe, out, aH, aL, bH, bL, first, last):
            pe.matmul(out, aH, bH, start=first, stop=False)
            pe.matmul(out, aH, bL, start=False, stop=False)
            return pe.matmul(out, aL, bH, start=False, stop=last)

        def square(act, n, k):
            if k >= 3:
                act.wait_ge(acc_r, n * (KT - 1) + k - 2)
            dst = rstd[:, :] if k == 0 else (upb[:, 0:TC] if k % 2 else cu[:, :])
            act.activation(dst, xT[:, k], ACT.Square).then_inc(sq_r, 1)

        def high_part(act, n, k):
            act.activation(actH[:, k], xT[:, k], ACT.Copy, scale=gains[:, ds(n * KT + k, 1)]).then_inc(act_h, 1)

        def add_square(dve, n, k):
            dve.wait_ge(sq_r, n * KT + k + 1)
            if k >= 2:
                dve.wait_ge(acc_r, n * (KT - 1) + k - 1)
            sq = upb[:, 0:TC] if k % 2 else cu[:, :]
            dve.tensor_tensor(rstd[:, :], rstd[:, :], sq, ALU.add).then_inc(acc_r, 1)

        def low_part(dve, n, k):
            dve.wait_ge(act_h, n * KT + k + 1)
            dve.scalar_tensor_tensor(actL[:, k], xT[:, k], gains[:, ds(n * KT + k, 1)],
                                     actH[:, k].bitcast(F32), ALU.mult, ALU.subtract).then_inc(act_l, 1)

        def mean_square(dve, n):
            dve.wait_ge(ssq_mm, n + 1)
            dve.tensor_scalar(ms[:, 0:NB], bank[6][:, 0:NB], 1.0 / D, EPS, ALU.mult, ALU.add).then_inc(ms_r, 1)
            dve.tensor_scalar(ms[0:DEC, NB:NB + 1], bank[6][0:DEC, NB:NB + 1], 1.0 / D, EPS,
                              ALU.mult, ALU.add).then_inc(ms_r, 1)

        def norm_pe(pe, n):
            pe.wait_ge(acc_r, (n + 1) * (KT - 1))
            for i, (t0, r) in enumerate(TOK):
                m = pe.matmul(bank[6][0:r, i:i + 1], rstd[:, t0:t0 + r], ones[:, 0:1], start=True, stop=True)
            m.then_inc(ssq_mm, 1)

        def norm_pool(pool, n):
            pool.wait_ge(ms_r, 2 * n + 2)
            pool.tensor_tensor(rt[:, :], ms[:, :], mhalf[:, :], ALU.pow).then_inc(rt_r, 1)

        def each_block(eng, body):
            body(0, 0, 0, P, "first")
            with eng.Fori(0, 3) as j:
                body(1, j * 2 + 1, j, P, "mid")
                body(0, j * 2 + 2, j + 1, P, "mid")
            body(1, 7, 3, P, "last")
            body(0, 8, 4, DEC, "sample")

        Z_LOADS = (5, 4)

        def cols(i, r):
            return slice(SOFF, SOFF + DEC) if r == DEC else ds(i * P, P)

        block = ctx.enter_context(nc.Block())

        @block.sync
        def _(sp):
            sp.dma_start(ident[:, :], I["consts"][:, CI:CI + P]).then_inc(const_in, 16)

            for n, (name, l) in enumerate([(f"{part}_norm", l) for l in range(DEPTH) for part in ("attn", "ffn")]):
                sp.dma_start(grows[n * KT:(n + 1) * KT, :], I[name][l].rearrange("(a b) -> a b", b=P)).then_inc(rows_in, 16)
            sp.dma_start(grows[2 * DEPTH * KT:, :], I["final_norm"].rearrange("(a b) -> a b", b=P)).then_inc(rows_in, 16)

            def load_x(par, t, src, r):
                wait(sp, xin_tp, t - 1)
                sp.dma_start(xin[0:r, par], src).then_inc((xin_in0, xin_in1)[par], 16)

            xp = I["x_prompt"][0].rearrange("(i p) d -> i p d", p=P)
            load_x(0, 0, xp[0], P)
            load_x(1, 1, xp[1], P)
            with sp.Fori(1, 4) as j:
                load_x(0, j * 2, xp[ds(j * 2, 1)].rearrange("o p d -> (o p) d"), P)
                load_x(1, j * 2 + 1, xp[ds(j * 2 + 1, 1)].rearrange("o p d -> (o p) d"), P)
            load_x(0, 8, I["x_sample"][0], DEC)

            with sp.Fori(0, DEPTH) as l:
                sp.wait_ge(x_done, l + 1)
                w_in = I["w_in"][l].rearrange("(k p) n -> p k n", p=P)

                def load_wz(g, c0, w):
                    sp.wait_ge(wz_l, l * 5 + g)
                    sp.dma_start(rawz[:, :, 0:w], w_in[:, :, ds(c0, w)]).then_inc(rz_in, 16)

                def store_z(g, c0, w):
                    for i, (t0, r) in enumerate(TOK):
                        sp.wait_ge(z_ev, l * 45 + g * 9 + i + 1)
                        sp.dma_start(z_dram[i * P:i * P + r, ds(c0, w)], zst[0:r, i % 3, 0:w]).then_inc(z_st[i % 3], 16)

                sp.dma_start(rawz[:, :, 0:ZA], w_in[:, :, 0:ZA]).then_inc(rz_in, 16)
                load_wz(1, ZA, ZB)
                store_z(0, 0, ZA)
                with sp.Fori(1, 4) as g:
                    load_wz(g + 1, g * ZB + ZA, ZB)
                    store_z(g, g * ZB + (ZA - ZB), ZB)
                store_z(4, 3 * ZB + ZA, ZB)

                for s in z_st:
                    sp.wait_ge(s, (l + 1) * 5 * 3 * 16)
                sp.dma_start(table[:, :], I["consts"]).then_inc(par_in, 16)
                for name, i0, s in (("conv_w", 0, 0), ("conv_w", 1, 0), ("conv_w", 2, 1)):
                    sp.dma_start(rows[44 * (i0 % 2):44 * (i0 % 2) + 44, s],
                                 I[name][l, i0].rearrange("(a b) -> a b", b=P)).then_inc(par_in, 16)
                sp.dma_start(rows[44:88, 1], I["conv_b"][l].rearrange("(a b) -> a b", b=P)).then_inc(par_in, 16)
                for i0 in range(2):
                    sp.dma_start(rows[44 * i0:44 * i0 + 44, 2],
                                 I["cache_conv"][l, 0, i0].rearrange("(a b) -> a b", b=P)).then_inc(par_in, 16)
                sp.dma_start(gw[:, :, :], I["gmlp_w"][l].rearrange("h i j -> i h j")).then_inc(par_in, 16)
                for h in range(4):
                    sp.dma_start(gbias[64 * (h % 2):64 * (h % 2) + 64, h // 2],
                                 I["gmlp_b"][l, h:h + 1, :].broadcast_to([64, P])).then_inc(par_in, 16)
                sp.dma_start(ggain[:, :], I["gmlp_norm"][ds(l, 1), :].broadcast_to([P, 256])).then_inc(par_in, 16)
                for h in range(2):
                    sp.dma_start(sink[64 * h:64 * h + 64, :],
                                 I["attn_sinks"][ds(l, 1), 4 * h:4 * h + 4].broadcast_to([64, 4])).then_inc(par_in, 16)
                sp.dma_start(gateb[:, :], I["mlstm_gate_b"][ds(l, 1), :].broadcast_to([P, 8])).then_inc(par_in, 16)
                sp.dma_start(ckin[:, :], I["cache_k"][l, 0].rearrange("t h d -> t (h d)")).then_inc(par_in, 16)
                sp.dma_start(stin[0:HD, :].rearrange("v (h k) -> v h k", k=HD),
                             I["state_C"][l, 0].rearrange("h v k -> v h k")).then_inc(par_in, 16)
                sp.dma_start(stin[HD:HD + 1, :], I["state_n"][l, 0:1].rearrange("o h k -> o (h k)")).then_inc(par_in, 16)

                def mixer(par, i, zi, r, kind):
                    wait(sp, S["blk_done"], (l * 9 + i - 1) if not (isinstance(i, int) and i < 2) else 0)
                    src = z_dram[NB * P:NB * P + DEC, :] if kind == "sample" else z_dram[ds(i * P, P), :]
                    sp.dma_start(zb[par][0:r, :], src).then_inc(z_in[par], 16)
                    if kind == "sample":
                        sp.wait_ge(S["blk_done"], l * 9 + 8)
                        settle(sp, settled)
                        sp.wait_ge(sto_r, l * 4 + 2)
                        settle(sp, settled)
                        for q, dst in ((B_K, "prompt_k"), (B_V, "prompt_v")):
                            sp.dma_start(O[dst][l, 0].rearrange("t h d -> t (h d)"), zb[1][:, q:q + P]).then_inc(kv_st, 16)
                        sp.dma_start(O["prompt_C"][l, 0].rearrange("h v k -> v h k"),
                                     stout[0:HD].rearrange("v a (h k) -> v (a h) k", k=HD)).then_inc(st_st, 16)
                        sp.dma_start(O["prompt_n"][l, 0:1].rearrange("o h k -> o (h k)"),
                                     stout[HD:HD + 1].rearrange("v a k -> v (a k)")).then_inc(st_st, 16)
                        sp.dma_start(O["prompt_m"][l, 0:1], mp[0:1, :]).then_inc(st_st, 16)
                        sp.wait_ge(st_st, l * 96 + 48)
                        sp.dma_start(mp[:, :], I["state_m"][l, 0:1, :].broadcast_to([P, 4])).then_inc(v_init, 16)
                        sp.dma_start(vprev[:, :], I["cache_v"][l, 0].rearrange("t h d -> t (h d)")).then_inc(v_init, 16)

                each_block(sp, mixer)
                sp.wait_ge(S["blk_done"], l * 9 + 9)
                settle(sp, settled)
                sp.wait_ge(sto_r, l * 4 + 4)
                settle(sp, settled)
                for q, dst in ((B_K, "sample_k"), (B_V, "sample_v")):
                    sp.dma_start(O[dst][l, 0].rearrange("t h d -> t (h d)"), zb[0][0:DEC, q:q + P]).then_inc(kv_st, 16)
                sp.dma_start(O["sample_gmlp_v"][l, 0], vn[0:DEC, :]).then_inc(gv_st, 16)
                sp.dma_start(O["sample_C"][l, 0].rearrange("h v k -> v h k"),
                             stout[0:HD].rearrange("v a (h k) -> v (a h) k", k=HD)).then_inc(st_st, 16)
                sp.dma_start(O["sample_n"][l, 0:1].rearrange("o h k -> o (h k)"),
                             stout[HD:HD + 1].rearrange("v a k -> v (a k)")).then_inc(st_st, 16)
                sp.dma_start(O["sample_m"][l, 0:1], mp[0:1, :]).then_inc(st_st, 16)
                sp.wait_ge(kv_st, l * 64 + 64)
                settle(sp, settled)
                sp.wait_ge(gv_st, l * 16 + 16)
                settle(sp, settled)
                sp.wait_ge(st_st, l * 96 + 96)
                settle(sp, settled)

                w_out, w_up, w_down = I["w_out"][l], I["w_up"][l].rearrange("(k p) n -> p k n", p=P), I["w_down"][l]
                loaded = {"n": 0}

                def load_w(s, slot, parts):
                    if not (isinstance(s, int) and s < 3):
                        sp.wait_ge(w_l, l * N_W + s - 2)
                    for k, (dst, src) in enumerate(parts):
                        sp.dma_start(dst, src).then_inc(raw_in[slot], 16)

                for m in range(KT):
                    t = raw[:, m % 3]
                    c = slice(m * P, m * P + P)
                    load_w(m, m % 3, [
                        (t[:, 0:2], w_out[0:256, c].rearrange("(k p) n -> p k n", p=P)),
                        (t[0:64, 2:6], w_out[256:512, c].rearrange("(k p) n -> p k n", p=64)),
                        (t[64:128, 2:6], w_out[512:768, c].rearrange("(k p) n -> p k n", p=64)),
                        (t[:, 6:8], w_out[768:1024, c].rearrange("(k p) n -> p k n", p=P))])

                def load_up(s, slot, f):
                    load_w(s, slot, [(raw[:, slot], w_up[:, :, ds(f * P, P)])])

                def load_down(s, slot, f):
                    load_w(s, slot, [(raw[:, slot].rearrange("p k n -> p (k n)"), w_down[ds(f * P, P), :])])

                for r, f in enumerate((0, NF, 1, NF + 1)):
                    load_up(KT + r, (KT + r) % 3, f)
                with sp.Fori(0, NG - 1) as n:
                    s = n * 6 + 12
                    load_up(s, 0, n * 2 + 2)
                    load_up(s + 1, 1, n * 2 + 2 + NF)
                    load_down(s + 2, 2, n * 2)
                    load_down(s + 3, 0, n * 2 + 1)
                    load_up(s + 4, 1, n * 2 + 3)
                    load_up(s + 5, 2, n * 2 + 3 + NF)
                load_down(N_W - 2, 0, NF - 2)
                load_down(N_W - 1, 1, NF - 1)

                sp.wait_ge(cvo_r, l + 1)
                for s, dst in ((0, "prompt_conv"), (1, "sample_conv")):
                    sp.dma_start(O[dst][l, 0].rearrange("r (a b) -> (r a) b", b=P), cvo[:, s]).then_inc(cvo_st, 16)
                sp.wait_ge(cvo_st, l * 32 + 32)
                settle(sp, settled)

            for i in range(NTOK):
                sp.wait_ge(y_ea, i + 1)
                sp.wait_ge(y_ev, i + 1)
                dst = O["y_sample"][0] if i == NB else O["y_prompt"][0, i * P:(i + 1) * P, :]
                sp.dma_start(dst, yst[0:TOK[i][1], i % 2]).then_inc((y_st0, y_st1)[i % 2], 16)
            sp.wait_ge(y_st0, 80)
            sp.wait_ge(y_st1, 64)

        @block.tensor
        def _(pe):
            pe.wait_ge(const_in, 16)

            def turn_x(par, t, n, r):
                pe.wait_ge((xin_in0, xin_in1)[par], n * 16)
                wait(pe, xin_ea, t - 1)
                wait(pe, xin_ev, t - 1)
                for k in range(KT):
                    m = pe.transpose(bank[2 * par + k // 4][:, (k % 4) * P:(k % 4) * P + r],
                                     xin[0:r, par, k * P:(k + 1) * P], ident[0:r, 0:r])
                m.then_inc(xin_tp, 1)

            turn_x(0, 0, 1, P)
            turn_x(1, 1, 1, P)
            with pe.Fori(1, 4) as j:
                turn_x(0, j * 2, j + 1, P)
                turn_x(1, j * 2 + 1, j + 1, P)
            turn_x(0, 8, 5, DEC)
            n = (2 * DEPTH + 1) * KT
            pe.wait_ge(rows_in, (2 * DEPTH + 1) * 16)
            pe.transpose(bank[7][:, 0:n], grows[0:n, :], ident[0:n, 0:n]).then_inc(rows_tp, 1)
            pe.wait_ge(s_ones, 3)
            norm_pe(pe, 0)

            with pe.Fori(0, DEPTH) as l:
                pe.wait_ge(x_done, l + 1)

                def z_group(g, par, w, u0):
                    pe.wait_ge(wz_l, l * 5 + g + 1)
                    for i, (t0, r) in enumerate(TOK):
                        if not (isinstance(g, int) and g == 0 and i < 6):
                            pe.wait_ge(z_ev, l * 45 + g * 9 + i - 5)
                        out = bank[(u0 + i) % 6][0:r, 0:w]
                        for k in range(KT):
                            if isinstance(g, int) and g == 0 and i == 0:
                                pe.wait_ge(act_l, l * (2 * KT) + k + 1)
                            m = split3(pe, out, actH[:, k, t0:t0 + r], actL[:, k, t0:t0 + r],
                                       wzH[par][:, k, 0:w], wzL[par][:, k, 0:w], k == 0, k == KT - 1)
                        m.then_inc(z_mm, 1)

                z_group(0, 0, ZA, 0)
                with pe.Fori(0, 2) as h:
                    z_group(h * 2 + 1, 1, ZB, 3)
                    z_group(h * 2 + 2, 0, ZB, 0)

                pe.wait_ge(par_in, (l + 1) * 304)
                pe.wait_ge(z_ev, l * 45 + 45)
                for h in range(4):
                    m = pe.transpose(bank[0][:, h * P:(h + 1) * P], gw[:, h], ident[:, :])
                m.then_inc(par_tp, 1)
                for s in range(3):
                    m = pe.transpose(bank[1][:, s * 88:s * 88 + 88], rows[:, s], ident[0:88, 0:88])
                m.then_inc(par_tp, 1)

                def mixer(par, i, zi, r, kind):
                    b1 = l * 9 + i + 1
                    c1 = l * 8 + i + 1
                    z = zb[par]
                    pe.wait_ge(z_in[par], (l * Z_LOADS[par] + zi + 1) * 16)
                    if kind == "first":
                        pe.wait_ge(gwT_r, l + 1)
                        pe.wait_ge(init_r, l * 9 + 9)
                    else:
                        pe.wait_ge(S["blk_done"], b1 - 1)
                    if kind == "sample":
                        pe.wait_ge(cn_r, l * 2 + 2)
                        pe.wait_ge(v_init, l * 32 + 32)
                    if r == DEC:
                        settle(pe, settled)
                    for s in range(4):
                        m = pe.transpose(bank[4][:, s * P:s * P + r], z[0:r, C_Q + s * P:C_Q + (s + 1) * P], ident[0:r, 0:r])
                    m.then_inc(S["tC_r"], 1)
                    for s in range(2):
                        pe.transpose(bank[5][:, s * P:s * P + r], z[0:r, A_U + s * P:A_U + (s + 1) * P], ident[0:r, 0:r])
                    pe.wait_ge(S["rope_r"], b1)
                    pe.wait_ge(S["qp_r"], b1)
                    if r == DEC:
                        settle(pe, settled)
                    pe.transpose(bank[5][:, 2 * P:2 * P + r], z[0:r, B_K:B_K + P], ident[0:r, 0:r]).then_inc(S["tU_r"], 1)
                    for s in range(4):
                        m = pe.transpose(bank[7][:, s * P:s * P + r], qp[0:r, s * P:(s + 1) * P], ident[0:r, 0:r])
                    m.then_inc(S["tB_r"], 1)
                    pe.wait_ge(S["lf_r"], b1)
                    if r == DEC:
                        settle(pe, settled)
                    pe.matmul(bank[6][0:r, 0:4], table[0:r, CU:CU + r], lf[0:r, :], start=True, stop=True)
                    pe.matmul(bank[6][:, 4:8], ones[0:r, :], lf[0:r, :], start=True, stop=True).then_inc(S["cum_r"], 1)
                    pe.wait_ge(S["cT_r"], b1)
                    if r == DEC:
                        settle(pe, settled)
                    for h in range(4):
                        m = pe.matmul(bank[4][0:r, h * P:h * P + r], qz[:, h, 0:r], ckT[:, h // 2, 0:r],
                                      start=True, stop=True)
                    m.then_inc(S["qk_r"], 1)
                    pe.wait_ge(S["bq_r"], b1)
                    pe.wait_ge(S["kT_r"], b1)
                    settle(pe, settled)
                    nch = 1 if kind == "sample" else 2
                    for c in range(nch):
                        k0, k1 = (128 if kind == "first" else 64 * c), 192 + 64 * c
                        for p in range(4):
                            for v in range(2):
                                m = pe.matmul(bank[2 * c + p // 2][64 * v:64 * v + 64, (p % 2) * 256 + k0:(p % 2) * 256 + k1],
                                              bqT[64 * v:64 * v + 64, p, 64 * c:64 * c + 64],
                                              kTw[64 * v:64 * v + 64, k0:k1], start=True, stop=True)
                        m.then_inc(S2["S_r"][c], 1)
                    pe.wait_ge(S["dA_r"], b1)
                    if r == DEC:
                        settle(pe, settled)
                    pe.matmul(bank[6][:, 0:4 * r], ones[0:r, :], dA[0:r, 0:4 * r], start=True, stop=True).then_inc(S["A_r"], 1)
                    pe.wait_ge(S["vn_r"], b1)
                    if r == DEC:
                        settle(pe, settled)
                    for h in range(4):
                        m = pe.matmul(bank[7][64 * (h % 2):64 * (h % 2) + 64, (h // 2) * P:(h // 2) * P + r],
                                      vn[0:r, h * 64:h * 64 + 64], gwT[0:r, h, 0:r], start=True, stop=True)
                    m.then_inc(S["mix_r"], 1)
                    for h in range(4):
                        m = pe.matmul(bank[5][0:r, h * 65:h * 65 + 65], qz[:, h, 0:r], CN[:, h // 2, :],
                                      start=True, stop=True)
                    m.then_inc(S["int_r"], 1)
                    for c in range(nch):
                        pe.wait_ge(S2["p_r"][c], b1 if c == 0 else c1)
                        for t in range(2):
                            for p in range(4):
                                m = pe.transpose(bank[2 * c + t][:, p * P:(p + 1) * P],
                                                 prob[c][:, p, t * P:(t + 1) * P], ident[:, :])
                        m.then_inc(S2["PT_r"][c], 1)
                    pe.wait_ge(S["W_r"], b1)
                    if r == DEC:
                        settle(pe, settled)
                    for h in range(4):
                        m = pe.transpose(bank[4][0:r, h * P:h * P + r], Wt[0:r, h, 0:r], ident[0:r, 0:r])
                    m.then_inc(S["WT_r"], 1)
                    pe.wait_ge(S["mA_r"], b1)
                    for c in range(nch):
                        pe.wait_ge(S2["pTa_r"][c], b1 if c == 0 else c1)
                        pe.wait_ge(S2["pTv_r"][c], b1 if c == 0 else c1)
                        for v in range(2):
                            for t in range(2):
                                n = DEC if (kind == "sample" and t == 1) else P
                                vt = z[0:n, B_V + 64 * v:B_V + 64 * v + 64] if t else vprev[:, 64 * v:64 * v + 64]
                                m = pe.matmul(bank[7][64 * v:64 * v + 64, 0:512].rearrange("d (p q) -> d p q", p=4)[:, :, 64 * c:64 * c + 64],
                                              vt, pT[c][0:n, t, :, 64 * v:64 * v + 64], start=(t == 0), stop=(t == 1))
                    m.then_inc(S["pv_r"], 1)
                    pe.wait_ge(S["WTs_r"], b1)
                    pe.wait_ge(S["vx_r"], b1)
                    pe.wait_ge(S["A_used"], b1)
                    if r == DEC:
                        settle(pe, settled)
                    for h in range(4):
                        m = pe.matmul(bank[6][0:r, h * 65:h * 65 + 65], WTs[0:r, h, 0:r], Vx[0:r, h, :], start=True, stop=True)
                    m.then_inc(S["num_r"], 1)
                    pe.wait_ge(S["kw_r"], b1)
                    if r == DEC:
                        settle(pe, settled)
                    for h in range(4):
                        m = pe.matmul(bank[4][64 * (h % 2):64 * (h % 2) + 64, (h // 2) * 65:(h // 2) * 65 + 65],
                                      kw[0:r, h * 64:h * 64 + 64], Vx[0:r, h, :], start=True, stop=True)
                    m.then_inc(S["kwmm_r"], 1)
                    pe.wait_ge(S["hc_r"], b1)
                    if r == DEC:
                        settle(pe, settled)
                    for s in range(2):
                        m = pe.transpose(bank[5][:, s * P:s * P + r], hc[0:r, s * P:(s + 1) * P], ident[0:r, 0:r])
                    m.then_inc(S["hT_r"], 1)
                    if kind in ("last", "sample"):
                        first = kind == "last"
                        pe.wait_ge(S["blk_done"], b1)
                        for s in range(2):
                            m = pe.transpose(bank[s][0:HD + 1, 0:P], CN[:, s, :], ident[:, :])
                        m.then_inc(stt_r, 1)
                        if first:
                            pe.transpose(bank[2][:, 0:P], ckin[:, :], ident[:, :]).then_inc(ck_r, 1)
                            for s in range(2):
                                m = pe.transpose(bank[3][:, s * 65:s * 65 + 65], stin[:, s * P:(s + 1) * P], ident[0:65, 0:65])
                            m.then_inc(ck_r, 1)

                each_block(pe, mixer)

                def set_use(u, s, c, w):
                    if not (isinstance(u, int) and u < 2):
                        pe.wait_ge(bank_free, l * (3 * N_USE) + (u - 2) * 3 + (c + 1))
                    return bank[3 * s + c][:, 0:w]

                def weights(s, slot, n=1):
                    pe.wait_ge(w_l, l * N_W + s + n)
                    return wH[:, slot], wL[:, slot]

                def product(u, uset, s, slot, fresh=False):
                    h, lo = weights(s, slot)
                    for c, (t0, w) in enumerate(CH):
                        out = set_use(u, uset, c, w)
                        for k in range(KT):
                            if fresh and c == 0:
                                pe.wait_ge(act_l, l * (2 * KT) + KT + k + 1)
                            m = split3(pe, out, h[:, k], lo[:, k], actH[:, k, t0:t0 + w], actL[:, k, t0:t0 + w],
                                       k == 0, k == KT - 1)
                        m.then_inc(mm, 1)

                pe.wait_ge(S["blk_done"], l * 9 + 9)
                for m in range(KT):
                    product(m, m % 2, m, m % 6)
                norm_pe(pe, l * 2 + 1)
                product(KT, 0, KT, KT % 6, fresh=True)
                pe.wait_ge(diag_r, l + 1)
                pe.wait_ge(bank_free, l * (3 * N_USE) + 3 * KT)
                for s in range(3):
                    n = 3 if s < 2 else 2
                    m = pe.matmul(bank[3 + s][:, 0:n * P], ones[:, :], diag[:, 3 * s:3 * s + n], start=True, stop=True)
                m = pe.matmul(bank[5][:, 2 * P:2 * P + DEC], ones[0:DEC, :], diag[0:DEC, NB, 0:DEC], start=True, stop=True)
                m.then_inc(rs_mm, 1)
                pe.wait_ge(rstd_r, l * 5 + 5)
                for r in range(1, 4):
                    product(KT + r, r % 2, KT + r, (KT + r) % 6)

                def down(n, u, s, par):
                    pe.wait_ge(g_l, l * NF + n * 2 + 2)
                    weights(s, 2, 2)
                    for m in range(KT):
                        for c, (t0, w) in enumerate(CH):
                            out = set_use(u + m, m % 2, c, w)
                            for t, slot in enumerate((par, 2)):
                                h = wH[:, 2 + t].rearrange("p k n -> p (k n)")[:, m * P:(m + 1) * P]
                                lo = wL[:, 2 + t].rearrange("p k n -> p (k n)")[:, m * P:(m + 1) * P]
                                q = split3(pe, out, h, lo, gHL[:, slot, 0, t0:t0 + w], gHL[:, slot, 1, t0:t0 + w],
                                           t == 0, t == 1)
                            q.then_inc(mm, 1)

                def group(n, par):
                    s, u = n * 6 + 12, n * 12 + 12
                    product(u, 0, s, 0)
                    product(u + 1, 1, s + 1, 1)
                    down(n, u + 2, s + 2, par)
                    product(u + 10, 0, s + 4, 4)
                    product(u + 11, 1, s + 5, 5)

                with pe.Fori(0, (NG - 1) // 2) as j:
                    group(j * 2, 0)
                    group(j * 2 + 1, 1)
                pe.wait_ge(g_l, l * NF + NF)
                weights(N_W - 2, 0, 2)
                for m in range(KT):
                    for c, (t0, w) in enumerate(CH):
                        out = set_use(N_USE - KT + m, m % 2, c, w)
                        for t, slot in enumerate((0, 2)):
                            h = wH[:, t].rearrange("p k n -> p (k n)")[:, m * P:(m + 1) * P]
                            lo = wL[:, t].rearrange("p k n -> p (k n)")[:, m * P:(m + 1) * P]
                            q = split3(pe, out, h, lo, gHL[:, slot, 0, t0:t0 + w], gHL[:, slot, 1, t0:t0 + w],
                                       t == 0, t == 1)
                        q.then_inc(mm, 1)
                pe.wait_ge(cvs_r, (l + 1) * 4 * NF)
                for s in range(2):
                    m = pe.transpose(bank[7][0:88, s * P:(s + 1) * P],
                                     convst[:, 2 * s:2 * s + 2].rearrange("p r a -> p (r a)"), ident[:, :])
                m.then_inc(cvt_r, 1)
                norm_pe(pe, l * 2 + 2)

            pe.wait_ge(identr_r, 1)
            pe.wait_ge(act_l, (2 * DEPTH + 1) * KT)
            for i, (t0, r) in enumerate(TOK):
                wait(pe, y_ea, i - 1)
                wait(pe, y_ev, i - 1)
                for k in range(KT):
                    out = bank[2 * (i % 2) + k // 4][0:r, (k % 4) * P:(k % 4 + 1) * P]
                    pe.matmul(out, actH[:, k, t0:t0 + r], identr[:, :], start=True, stop=False)
                    m = pe.matmul(out, actL[:, k, t0:t0 + r], identr[:, :], start=False, stop=True)
                m.then_inc(y_tp, 1)

        @block.scalar
        def _(act):
            def turn_x(par, t, c0, r):
                act.wait_ge(xin_tp, t + 1)
                act.activation(xT[:, 0:4, c0], bank[2 * par][:, :].rearrange("p (k t) -> p k t", k=4)[:, :, 0:r],
                               ACT.Copy).then_inc(xin_ea, 1)

            turn_x(0, 0, ds(0, P), P)
            turn_x(1, 1, ds(P, P), P)
            with act.Fori(1, 4) as j:
                turn_x(0, j * 2, ds(j * 256, P), P)
                turn_x(1, j * 2 + 1, ds(j * 256 + P, P), P)
            turn_x(0, 8, slice(SOFF, TC), DEC)

            act.wait_ge(rows_tp, 1)
            act.activation(gains[:, :], bank[7][:, 0:(2 * DEPTH + 1) * KT], ACT.Copy).then_inc(gains_r, 1)
            act.wait_ge(gains_r, 1)
            act.wait_ge(x_done, 1)
            for k in range(KT):
                square(act, 0, k)
                high_part(act, 0, k)

            with act.Fori(0, DEPTH) as l:
                def split_wz(g, par, w):
                    act.wait_ge(rz_in, (l * 5 + g + 1) * 16)
                    if not (isinstance(g, int) and g < 2):
                        act.wait_ge(z_mm, l * 45 + (g - 1) * 9)
                    act.activation(wzH[par][:, :, 0:w], rawz[:, :, 0:w], ACT.Copy).then_inc(wz_h, 1)

                def evac_z(g, w, u0, func):
                    for i, (t0, r) in enumerate(TOK):
                        act.wait_ge(z_mm, l * 45 + g * 9 + i + 1)
                        if not (isinstance(g, int) and g == 0 and i < 3):
                            act.wait_ge(z_st[i % 3], (l * 15 + g * 3 + i // 3) * 16)
                        act.activation(zst[0:r, i % 3, 0:w], bank[(u0 + i) % 6][0:r, 0:w], func,
                                       scale=rt[0:r, i:i + 1]).then_inc(z_ev, 1)

                split_wz(0, 0, ZA)
                split_wz(1, 1, ZB)
                act.wait_ge(rt_r, l * 2 + 1)
                evac_z(0, ZA, 0, ACT.Gelu)
                for g in range(1, 5):
                    if g < 4:
                        split_wz(g + 1, (g + 1) % 2, ZB)
                    evac_z(g, ZB, 3 * (g % 2), ACT.Copy)

                act.wait_ge(par_tp, l * 2 + 1)
                t = bank[0][:, :].rearrange("p (h i) -> p h i", h=4)
                act.activation(gwT[0:64], t[0:64], ACT.Copy)
                act.activation(gwT[64:128, :, 64:128], t[64:128, :, 64:128], ACT.Copy).then_inc(gwT_r, 1)
                act.wait_ge(par_tp, l * 2 + 2)
                act.activation(convc[:, :], bank[1][:, 0:264], ACT.Copy).then_inc(conv_r, 1)

                def mixer(par, i, zi, r, kind):
                    b1 = l * 9 + i + 1
                    c1 = l * 8 + i + 1
                    z = zb[par]
                    nch = 1 if kind == "sample" else 2
                    act.wait_ge(z_in[par], (l * Z_LOADS[par] + zi + 1) * 16)
                    if kind != "first":
                        act.wait_ge(S["blk_done"], b1 - 1)
                    act.wait_ge(S["rope_r"], b1)
                    act.activation(qp[0:r].rearrange("t (p v d) -> t p v d", p=4, v=2),
                                   z[0:r, B_Q:B_Q + 512].rearrange("t (v p d) -> t p v d", p=4, v=2), ACT.Copy).then_inc(S["qp_r"], 1)
                    act.wait_ge(S["tC_r"], b1)
                    t = bank[4][:, :].rearrange("p (s t) -> p s t", s=4)
                    for v in range(2):
                        act.activation(qz[64 * v:64 * v + 64].rearrange("p (s v) t -> p s v t", v=2)[:, :, v, 0:r],
                                       t[64 * v:64 * v + 64, 0:2, 0:r], ACT.Copy)
                    act.activation(ckT[:, :, 0:r], t[:, 2:4, 0:r], ACT.Copy, scale=SCALE).then_inc(S["cT_r"], 1)
                    act.wait_ge(S["ax_r"], b1)
                    act.activation(ax[0:r], ax[0:r], ACT.Exp, scale=-1.0).then_inc(act_seq, 1)
                    act.wait_ge(act_seq, b1)
                    act.activation(ax[0:r], ax[0:r], ACT.Ln, bias=1.0).then_inc(S["lg_r"], 1)
                    act.wait_ge(S["tU_r"], b1)
                    t = bank[5][:, 0:3 * P].rearrange("p (s t) -> p s t", s=3)
                    act.activation(uT[:, :, 0:r], t[:, 0:2, 0:r], ACT.Copy)
                    act.activation(kTw[:, P:P + r], bank[5][:, 2 * P:2 * P + r], ACT.Copy).then_inc(S["kT_r"], 1)
                    for c in range(nch):
                        k0, k1 = (128 if kind == "first" else 64 * c), 192 + 64 * c
                        act.wait_ge(S2["nm_r"][c], b1 if c == 0 else c1)
                        for p in range(4):
                            act.activation(prob[c][:, p, k0:k1], bank[2 * c + p // 2][:, (p % 2) * 256 + k0:(p % 2) * 256 + k1],
                                           ACT.Exp, bias=nm[:, c, p:p + 1], scale=SCALE, accum_out=rs[:, c, p:p + 1])
                        act.activation(es[:, c], es[:, c], ACT.Exp).then_inc(S2["e_r"][c], 1)
                    act.wait_ge(S["sm_r"], b1)
                    act.activation(ex[:, :], sm[:, :], ACT.Exp).then_inc(S["ex_r"], 1)
                    act.wait_ge(S["D_r"], b1)
                    act.activation(Am[0:r, :, 0:r], Am[0:r, :, 0:r], ACT.Exp).then_inc(S["P_r"], 1)
                    act.activation(eo[0:r], z[0:r, C_O:C_O + 256], ACT.Exp, scale=-1.0).then_inc(S["eo_r"], 1)
                    for c in range(nch):
                        act.wait_ge(S2["PT_r"][c], b1 if c == 0 else c1)
                        act.activation(pT[c][:, 1], bank[2 * c + 1][:, :].rearrange("p (s t) -> p s t", s=4),
                                       ACT.Copy).then_inc(S2["pTa_r"][c], 1)
                    act.wait_ge(S["WT_r"], b1)
                    act.activation(WTs[0:r, :, 0:r], bank[4][0:r, :].rearrange("p (s t) -> p s t", s=4)[:, :, 0:r],
                                   ACT.Copy).then_inc(S["WTs_r"], 1)
                    cc = cols(i, r)
                    act.wait_ge(S["mA_r"], b1)
                    act.activation(actH[:, 0:2, cc], mixA[:, :, 0:r], ACT.Copy).then_inc(S["hA_r"], 1)
                    act.wait_ge(S["pv_r"], b1)
                    act.activation(actH[:, 2:6, cc], bank[7][:, :].rearrange("p (s t) -> p s t", s=4)[:, :, 0:r],
                                   ACT.Copy).then_inc(S["hB_r"], 1)
                    act.wait_ge(S["hT_r"], b1)
                    act.activation(actH[:, 6:8, cc], bank[5][:, 0:2 * P].rearrange("p (s t) -> p s t", s=2)[:, :, 0:r],
                                   ACT.Copy).then_inc(S["hC_r"], 1)
                    if kind in ("last", "sample"):
                        act.wait_ge(stt_r, l * 2 + (1 if kind == "last" else 2))
                        if kind == "sample":
                            act.wait_ge(st_st, l * 96 + 48)
                        for s in range(2):
                            act.activation(stout[:, s], bank[s][0:HD + 1, 0:P], ACT.Copy).then_inc(sto_r, 1)
                        if kind == "last":
                            act.wait_ge(ck_r, l * 2 + 2)
                            act.activation(kTw[:, 0:P], bank[2][:, 0:P], ACT.Copy).then_inc(cn_r, 1)
                            act.activation(CN[:, :, :], bank[3][:, 0:130].rearrange("p (s k) -> p s k", s=2),
                                           ACT.Copy).then_inc(cn_r, 1)

                each_block(act, mixer)

                M0 = l * (3 * N_USE)

                def split_w(s, slot, rslot, count, done):
                    act.wait_ge(raw_in[rslot], l * RAW_PER[rslot] + count)
                    if done is not None:
                        act.wait_ge(mm, M0 + done)
                    act.activation(wH[:, slot], raw[:, rslot], ACT.Copy).then_inc(w_h, 1)

                act.wait_ge(S["blk_done"], l * 9 + 9)
                for s in range(6):
                    split_w(s, s, s % 3, RAW_AT[s], None)
                for m in range(KT):
                    split_w(m + 6, (m + 6) % 6, m % 3, RAW_AT[m + 6], 3 * (m + 1))
                    act.wait_ge(bank_free, M0 + 3 * (m + 1))
                    square(act, l * 2 + 1, m)
                for k in range(KT):
                    high_part(act, l * 2 + 1, k)

                def up_tile(q, f, slot):
                    act.wait_ge(up_r, l * (2 * NF) + q + 1)
                    if slot is None and not (isinstance(q, int) and q == 0):
                        act.wait_ge(g_l, l * NF + half(q))
                    if slot is not None:
                        act.wait_ge(gelu_r, l * NF + half(q - 1) + 1)
                    act.activation(cv[:, :], upb[:, PAD:], ACT.Identity, scale=convc[:, ds(f + 88, 1)],
                                   bias=convc[:, ds(f + 132, 1)]).then_inc(c0_r, 1)
                    if slot is None:
                        act.wait_ge(tap_r, l * (2 * NF) + q + 1)
                        act.activation(cu[:, :], cv[:, :], ACT.Gelu).then_inc(gelu_r, 1)
                    else:
                        act.wait_ge(gmul_r, l * NF + half(q - 1) + 1)
                        act.activation(gHL[:, slot, 0], cv[:, :], ACT.Copy).then_inc(g_h, 1)

                act.wait_ge(rstd_r, l * 5 + 5)
                for r, (f, slot) in enumerate(((0, None), (NF, 0), (1, None), (NF + 1, 2))):
                    up_tile(r, f, slot)
                    split_w(14 + r, 2 + r, (2 + r) % 3, RAW_AT[14 + r], 3 * (KT + r + 1))

                def group(n, par, ahead):
                    u = n * 12 + 12
                    up_tile(n * 4 + 4, n * 2 + 2, None)
                    split_ahead(n, 0, u * 3 + 3)
                    up_tile(n * 4 + 5, n * 2 + 2 + NF, 1 - par)
                    split_ahead(n, 1, u * 3 + 6)
                    if ahead:
                        split_ahead(n, 2, u * 3 + 30)
                        split_ahead(n, 3, u * 3 + 30)
                    up_tile(n * 4 + 6, n * 2 + 3, None)
                    if ahead:
                        split_ahead(n, 4, u * 3 + 33)
                    up_tile(n * 4 + 7, n * 2 + 3 + NF, 2)
                    if ahead:
                        split_ahead(n, 5, u * 3 + 36)

                def split_ahead(n, r, done):
                    split_w(n * 6 + 18 + r, r, r % 3, n * 32 + (RAW_12[r % 3] + 32 + 16 * (r // 3 + 1)), done)

                with act.Fori(0, (NG - 3) // 2) as j:
                    group(j * 2, 0, True)
                    group(j * 2 + 1, 1, True)
                group(NG - 3, 0, True)
                group(NG - 2, 1, False)
                for m in range(KT):
                    act.wait_ge(bank_free, M0 + 3 * (N_USE - KT + m + 1))
                    square(act, l * 2 + 2, m)
                    high_part(act, l * 2 + 2, m)
                act.wait_ge(cvt_r, l + 1)
                act.activation(cvo[:, :, :], bank[7][0:88, 0:256].rearrange("p (s t) -> p s t", s=2), ACT.Copy).then_inc(cvo_r, 1)

            act.wait_ge(x_done, DEPTH + 1)
            act.activation(identr[:, :], ident[:, :], ACT.Copy).then_inc(identr_r, 1)
            act.wait_ge(rt_r, 2 * DEPTH + 1)
            for i, (t0, r) in enumerate(TOK):
                act.wait_ge(y_tp, i + 1)
                wait(act, (y_st0, y_st1)[i % 2], 16 * (i // 2))
                act.activation(yst[0:r, i % 2, 0:512], bank[2 * (i % 2)][0:r, :], ACT.Copy, scale=rt[0:r, i:i + 1]).then_inc(y_ea, 1)

        @block.gpsimd
        def _(pool):
            pool.memset(ones[:, :], 1.0).then_inc(s_ones, 1)
            pool.memset(ms[:, :], 1.0).then_inc(s_ones, 1)
            pool.memset(mhalf[:, :], -0.5).then_inc(s_ones, 1)
            pool.wait_ge(s_ones, 3)
            norm_pool(pool, 0)
            with pool.Fori(0, DEPTH) as l:
                pool.wait_ge(par_in, (l + 1) * 304)
                settle(pool, settled)
                for t in (prob[0][:, :, :], prob[1][:, :, :], CN[:, :, :], qz[:, :, :], mp[:, :], vprev[:, :], kTw[:, 0:P]):
                    pool.memset(t, 0.0).then_inc(init_r, 1)
                pool.memset(Vx[:, :, HD:HD + 1], 1.0).then_inc(init_r, 1)

                def mixer(par, i, zi, r, kind):
                    b1 = l * 9 + i + 1
                    z = zb[par]
                    pool.wait_ge(z_in[par], (l * Z_LOADS[par] + zi + 1) * 16)
                    if kind == "first":
                        pool.wait_ge(init_r, l * 9 + 9)
                    else:
                        pool.wait_ge(S["blk_done"], b1 - 1)
                    qk = z[0:r, B_Q:B_Q + 640].rearrange("t (h d) -> t h d", h=10)
                    co = table[0:r, ds(i * ROT + CCOS, ROT)].rearrange("t (o d) -> t o d", o=1)
                    si = table[0:r, ds(i * ROT + CSIN, ROT)].rearrange("t (o d) -> t o d", o=1)
                    pool.tensor_tensor(rp1[0:r], qk[:, :, 0:ROT], co.broadcast_to([r, 10, ROT]), ALU.mult)
                    pool.tensor_tensor(rp2[0:r, :, 0:8], qk[:, :, 8:16], si[:, :, 0:8].broadcast_to([r, 10, 8]), ALU.mult)
                    pool.tensor_tensor(rp2[0:r, :, 8:16], qk[:, :, 0:8], si[:, :, 8:16].broadcast_to([r, 10, 8]),
                                       ALU.mult).then_inc(rp_r, 1)
                    pool.wait_ge(rp_r, b1)
                    pool.tensor_tensor(qk[:, :, 0:ROT], rp1[0:r], rp2[0:r], ALU.add).then_inc(S["rope_r"], 1)
                    pool.tensor_copy(Vx[0:r, :, 0:HD], z[0:r, C_V:C_V + 256].rearrange("t (h d) -> t h d", h=4)).then_inc(S["vx_r"], 1)
                    pool.wait_ge(S["vms_r"], b1)
                    pool.tensor_tensor(rv[0:r], vss[0:r], mhalf[0:r, 0:1], ALU.pow).then_inc(S["rv_r"], 1)
                    pool.wait_ge(S["pv_r"], b1)
                    settle(pool, settled)
                    if kind in ("first", "mid"):
                        pool.tensor_copy(vprev[:, :], z[:, B_V:B_V + P])
                        pool.tensor_copy(kTw[:, 0:P], kTw[:, P:2 * P]).then_inc(S["keep_r"], 1)
                    else:
                        pool.memset(rp1[:, 0, 0:1], 0.0).then_inc(S["keep_r"], 1)

                each_block(pool, mixer)
                norm_pool(pool, l * 2 + 1)
                norm_pool(pool, l * 2 + 2)

        @block.vector
        def _(dve):
            def turn_x(par, t, c0, r):
                dve.wait_ge(xin_tp, t + 1)
                dve.tensor_copy(xT[:, 4:8, c0], bank[2 * par + 1][:, :].rearrange("p (k t) -> p k t", k=4)[:, :, 0:r]).then_inc(xin_ev, 1)

            dve.memset(xT[:, :, SEQ:SOFF], 0.0)
            turn_x(0, 0, ds(0, P), P)
            turn_x(1, 1, ds(P, P), P)
            with dve.Fori(1, 4) as j:
                turn_x(0, j * 2, ds(j * 256, P), P)
                turn_x(1, j * 2 + 1, ds(j * 256 + P, P), P)
            turn_x(0, 8, slice(SOFF, TC), DEC)
            dve.wait_ge(xin_ea, NTOK)
            dve.wait_ge(xin_ev, NTOK)
            dve.wait_ge(s_ones, 3)
            dve.memset(cu[:, 0:1], 0.0).then_inc(x_done, 1)
            dve.wait_ge(gains_r, 1)
            low_part(dve, 0, 0)
            for k in range(1, KT):
                add_square(dve, 0, k)
                low_part(dve, 0, k)
            mean_square(dve, 0)

            with dve.Fori(0, DEPTH) as l:
                def split_wz(g, par, w):
                    dve.wait_ge(wz_h, l * 5 + g + 1)
                    dve.tensor_tensor(wzL[par][:, :, 0:w], rawz[:, :, 0:w], wzH[par][:, :, 0:w].bitcast(F32),
                                      ALU.subtract).then_inc(wz_l, 1)

                split_wz(0, 0, ZA)
                for g in range(1, 5):
                    split_wz(g, g % 2, ZB)

                dve.wait_ge(par_in, (l + 1) * 304)
                dve.tensor_scalar(nsink[:, :], sink[:, :], -1.0, None, ALU.mult)
                dve.memset(sm[:, :], 0.0)
                dve.memset(gwT[64:128, :, 0:64], 0.0).then_inc(init_r, 1)

                def mixer(par, i, zi, r, kind):
                    b1 = l * 9 + i + 1
                    c1 = l * 8 + i + 1
                    z = zb[par]
                    nch = 1 if kind == "sample" else 2
                    base = l * (8 * LINKS + LINKS_SAMPLE) + i * LINKS
                    ch = Chain(dve, mix_seq, base)
                    link = ch.link

                    def flag(ins, s, n=b1):
                        ins.then_inc(s, 1)
                        dve.wait_ge(s, n)

                    def row(t, n, m):
                        return t.rearrange("p (h o) -> p h o", o=1).broadcast_to([t.shape[0], n, m])

                    dve.wait_ge(z_in[par], (l * Z_LOADS[par] + zi + 1) * 16)
                    if kind == "first":
                        dve.wait_ge(init_r, l * 9 + 9)
                    link(dve.tensor_tensor(g8[0:r], z[0:r, C_G:C_G + 8], gateb[0:r], ALU.add))
                    dve.scalar_tensor_tensor(ax[0:r], g8[0:r, 4:8], -1.0, g8[0:r, 4:8], ALU.mult, ALU.max).then_inc(S["ax_r"], 1)
                    link(dve.tensor_tensor(vsq[0:r], z[0:r, A_V:A_V + 256], z[0:r, A_V:A_V + 256], ALU.mult))
                    link(dve.tensor_reduce(vss[0:r], vsq[0:r], AX.X, ALU.add))
                    dve.tensor_scalar(vss[0:r], vss[0:r], 1.0 / 256, EPS, ALU.mult, ALU.add).then_inc(S["vms_r"], 1)
                    dve.wait_ge(S["lg_r"], b1)
                    flag(dve.scalar_tensor_tensor(lf[0:r], g8[0:r, 4:8], 0.0, ax[0:r], ALU.min, ALU.subtract), S["lf_r"])
                    dve.wait_ge(S["rv_r"], b1)
                    dve.scalar_tensor_tensor(vn[0:r], z[0:r, A_V:A_V + 256], rv[0:r], ggain[0:r],
                                             ALU.mult, ALU.mult).then_inc(S["vn_r"], 1)
                    dve.wait_ge(S["tB_r"], b1)
                    dve.tensor_copy(bqT[:, :, 0:r], bank[7][:, :].rearrange("p (s t) -> p s t", s=4)[:, :, 0:r]).then_inc(S["bq_r"], 1)
                    dve.wait_ge(S["cum_r"], b1)
                    dve.tensor_copy(bb[0:r, 0:4], bank[6][0:r, 0:4])
                    link(dve.tensor_copy(bb[:, 4:8], bank[6][:, 4:8]))
                    link(dve.tensor_tensor(aa[0:r], g8[0:r, 0:4], bb[0:r, 0:4], ALU.subtract))
                    dve.tensor_tensor(dA[0:r, 0:4 * r].rearrange("p (h s) -> p h s", h=4),
                                      ident[0:r, 0:r].rearrange("p (o s) -> p o s", o=1).broadcast_to([r, 4, r]),
                                      row(aa[0:r], 4, r), ALU.mult).then_inc(S["dA_r"], 1)
                    for c in range(nch):
                        k0, k1 = (128 if kind == "first" else 64 * c), 192 + 64 * c
                        dve.wait_ge(S2["S_r"][c], b1 if c == 0 else c1)
                        for h in range(2):
                            t = dve.tensor_reduce(mx[:, c, 2 * h:2 * h + 2],
                                                  bank[2 * c + h][:, :].rearrange("p (s t) -> p s t", s=2)[:, :, k0:k1], AX.X, ALU.max)
                        link(t)
                        link(dve.scalar_tensor_tensor(nm[:, c], mx[:, c], -SCALE, nsink[:, :], ALU.mult, ALU.min))
                        dve.tensor_tensor(es[:, c], sink[:, :], nm[:, c], ALU.add).then_inc(S2["nm_r"][c], 1)
                    dve.wait_ge(S["A_r"], b1)
                    if kind == "sample":
                        dve.wait_ge(v_init, l * 32 + 32)
                    A = bank[6][:, 0:4 * r].rearrange("p (h s) -> p h s", h=4)
                    link(dve.tensor_tensor(Am[0:r, :, 0:r], A[0:r],
                                           table[0:r, CM:CM + r].rearrange("p (o s) -> p o s", o=1).broadcast_to([r, 4, r]), ALU.add))
                    dve.tensor_reduce(cm[0:r], Am[0:r, :, 0:r], AX.X, ALU.max)
                    flag(dve.tensor_reduce(G[:, :], A, AX.X, ALU.max), S["A_used"])
                    dve.tensor_tensor(cm[0:r], cm[0:r], mp[0:r], ALU.max)
                    link(dve.tensor_tensor(G[:, :], G[:, :], mp[:, :], ALU.max))
                    dve.tensor_tensor(sm[0:r, 0:4], mp[0:r], cm[0:r], ALU.subtract)
                    dve.scalar_tensor_tensor(sm[0:r, 4:8], bb[0:r, 0:4], -1.0, cm[0:r], ALU.mult, ALU.subtract)
                    dve.tensor_tensor(sm[0:r, 8:12], aa[0:r], G[0:r], ALU.subtract)
                    flag(dve.tensor_tensor(sm[:, 12:16], mp[:, :], G[:, :], ALU.subtract), S["sm_r"])
                    dve.tensor_tensor(mp[:, :], bb[:, 4:8], G[:, :], ALU.add)
                    dve.tensor_tensor(Am[0:r, :, 0:r], Am[0:r, :, 0:r], row(cm[0:r], 4, r), ALU.subtract).then_inc(S["D_r"], 1)
                    for c in range(nch):
                        k0, k1 = (128 if kind == "first" else 64 * c), 192 + 64 * c
                        dve.wait_ge(S2["e_r"][c], b1 if c == 0 else c1)
                        link(dve.tensor_tensor(rs[:, c], rs[:, c], es[:, c], ALU.add))
                        link(dve.reciprocal(rs[:, c], rs[:, c]))
                        for p in range(4):
                            t = dve.tensor_scalar(prob[c][:, p, k0:k1], prob[c][:, p, k0:k1], rs[:, c, p:p + 1], None, ALU.mult)
                        t.then_inc(S2["p_r"][c], 1)
                    dve.wait_ge(S["mix_r"], b1)
                    dve.wait_ge(S["kT_r"], b1)
                    link(dve.tensor_tensor(mixA[:, :, 0:r], bank[7][:, 0:256].rearrange("p (s t) -> p s t", s=2)[:, :, 0:r],
                                           gbias[:, :, 0:r], ALU.add))
                    flag(dve.tensor_tensor(mixA[:, :, 0:r], mixA[:, :, 0:r], uT[:, :, 0:r], ALU.mult), S["mA_r"])
                    dve.wait_ge(S["P_r"], b1)
                    dve.wait_ge(S["qk_r"], b1)
                    dve.tensor_tensor(Wt[0:r, :, 0:r], bank[4][0:r, :].rearrange("p (s t) -> p s t", s=4)[:, :, 0:r],
                                      Am[0:r, :, 0:r], ALU.mult).then_inc(S["W_r"], 1)
                    dve.wait_ge(S["ex_r"], b1)
                    dve.scalar_tensor_tensor(kw[0:r].rearrange("p (h d) -> p h d", h=4), z[0:r, C_K:C_K + 256].rearrange("p (h d) -> p h d", h=4),
                                             SCALE, row(ex[0:r, 8:12], 4, HD), ALU.mult, ALU.mult).then_inc(S["kw_r"], 1)
                    for c in range(nch):
                        dve.wait_ge(S2["PT_r"][c], b1 if c == 0 else c1)
                        dve.tensor_copy(pT[c][:, 0], bank[2 * c][:, :].rearrange("p (s t) -> p s t", s=4)).then_inc(S2["pTv_r"][c], 1)
                    dve.wait_ge(S["int_r"], b1)
                    link(dve.tensor_tensor(nd[0:r], bank[5][0:r, 0:260].rearrange("p (h d) -> p h d", h=4),
                                           row(ex[0:r, 0:4], 4, HD + 1), ALU.mult))
                    dve.wait_ge(S["num_r"], b1)
                    link(dve.tensor_tensor(nd[0:r], nd[0:r], bank[6][0:r, 0:260].rearrange("p (h d) -> p h d", h=4), ALU.add))
                    den = nd[0:r, :, HD:HD + 1].rearrange("p h o -> p (h o)")
                    link(dve.scalar_tensor_tensor(dn[0:r], den, -1.0, den, ALU.mult, ALU.max))
                    link(dve.tensor_tensor(dn[0:r], dn[0:r], ex[0:r, 4:8], ALU.max))
                    dve.wait_ge(S["eo_r"], b1)
                    e4 = eo[0:r].rearrange("p (h d) -> p h d", h=4)
                    link(dve.scalar_tensor_tensor(e4, e4, 1.0, row(dn[0:r], 4, HD), ALU.add, ALU.mult))
                    link(dve.reciprocal(eo[0:r], eo[0:r]))
                    dve.tensor_tensor(hc[0:r].rearrange("p (h d) -> p h d", h=4), nd[0:r, :, 0:HD], e4, ALU.mult).then_inc(S["hc_r"], 1)
                    for h in range(2):
                        t = dve.tensor_copy(dec[64 * h:64 * h + 64, :],
                                            ex[64 * h:64 * h + 64, 12:16].rearrange("p (s h) -> p h s", h=2)[:, h])
                    link(t)
                    dve.wait_ge(S["kwmm_r"], b1)
                    for s in range(2):
                        t = dve.scalar_tensor_tensor(CN[:, s], CN[:, s], dec[:, s:s + 1], bank[4][:, s * 65:s * 65 + 65], ALU.mult, ALU.add)
                    link(t)
                    cc = cols(i, r)
                    dve.wait_ge(S["hA_r"], b1)
                    dve.tensor_tensor(actL[:, 0:2, cc], mixA[:, :, 0:r], actH[:, 0:2, cc].bitcast(F32), ALU.subtract)
                    dve.wait_ge(S["hB_r"], b1)
                    dve.tensor_tensor(actL[:, 2:6, cc], bank[7][:, :].rearrange("p (s t) -> p s t", s=4)[:, :, 0:r],
                                      actH[:, 2:6, cc].bitcast(F32), ALU.subtract)
                    dve.wait_ge(S["hC_r"], b1)
                    dve.wait_ge(S["keep_r"], b1)
                    dve.tensor_tensor(actL[:, 6:8, cc], bank[5][:, 0:2 * P].rearrange("p (s t) -> p s t", s=2)[:, :, 0:r],
                                      actH[:, 6:8, cc].bitcast(F32), ALU.subtract).then_inc(S["blk_done"], 1)
                    dve.wait_ge(S["blk_done"], b1)
                    settle(dve, settled)
                    assert ch.n == (LINKS_SAMPLE if kind == "sample" else LINKS), ch.n

                each_block(dve, mixer)
                dve.memset(actL[:, :, SEQ:SOFF].bitcast(F32), 0.0)
                dve.memset(actH[:, :, SEQ:SOFF].bitcast(F32), 0.0)

                M0 = l * (3 * N_USE)

                def split_w(s, slot, rslot):
                    dve.wait_ge(w_h, l * N_W + s + 1)
                    dve.tensor_tensor(wL[:, slot], raw[:, rslot], wH[:, slot].bitcast(F32), ALU.subtract).then_inc(w_l, 1)

                def add_x(u, m, uset):
                    for c, (t0, w) in enumerate(CH):
                        dve.wait_ge(mm, M0 + u * 3 + (c + 1))
                        t = dve.tensor_tensor(xT[:, m, t0:t0 + w], bank[3 * uset + c][:, 0:w], xT[:, m, t0:t0 + w], ALU.add)
                        t.then_inc(bank_free, 1)

                for s in range(6):
                    split_w(s, s, s % 3)
                for m in range(KT):
                    add_x(m, m, m % 2)
                    split_w(m + 6, (m + 6) % 6, m % 3)
                    if m:
                        add_square(dve, l * 2 + 1, m)
                mean_square(dve, l * 2 + 1)
                for k in range(KT):
                    low_part(dve, l * 2 + 1, k)
                dve.wait_ge(rt_r, l * 2 + 2)
                dve.tensor_tensor(diag[:, :, :], ident[:, :].rearrange("p (o s) -> p o s", o=1).broadcast_to([P, NTOK, P]),
                                  rt[:, :].rearrange("p (h o) -> p h o", o=1).broadcast_to([P, NTOK, P]), ALU.mult).then_inc(diag_r, 1)
                dve.wait_ge(rs_mm, l + 1)
                for s in range(2):
                    dve.tensor_copy(rstd[:, 384 * s:384 * s + 384], bank[3 + s][:, 0:384]).then_inc(rstd_r, 1)
                dve.tensor_copy(rstd[:, 768:1024], bank[5][:, 0:256]).then_inc(rstd_r, 1)
                dve.tensor_copy(rstd[:, SOFF:TC], bank[5][:, 256:320]).then_inc(rstd_r, 1)
                dve.memset(rstd[:, SEQ:SOFF], 0.0).then_inc(rstd_r, 1)
                dve.wait_ge(rstd_r, l * 5 + 5)
                dve.memset(upb[:, 0:PAD], 0.0)

                def up_tile(q, f, u, uset, slot, adds=None):
                    if slot is not None:
                        dve.wait_ge(tap_r, l * (2 * NF) + q)
                    for c, (t0, w) in enumerate(CH):
                        dve.wait_ge(mm, M0 + u * 3 + (c + 1))
                        dve.tensor_tensor(upb[:, PAD + t0:PAD + t0 + w], bank[3 * uset + c][:, 0:w], rstd[:, t0:t0 + w],
                                          ALU.mult).then_inc(bank_free, 1)
                    dve.wait_ge(bank_free, M0 + u * 3 + 3)
                    cache = convc[:, 176:264].rearrange("p (r a) -> p r a", r=2)
                    dve.tensor_copy(convst[:, 0:2, ds(f, 1)], upb[:, SEQ:SEQ + 2].rearrange("p (r o) -> p r o", o=1)).then_inc(cvs_r, 1)
                    dve.tensor_copy(convst[:, 2:4, ds(f, 1)], upb[:, TC:TC + 2].rearrange("p (r o) -> p r o", o=1)).then_inc(cvs_r, 1)
                    dve.tensor_copy(upb[:, SOFF:SOFF + 2].rearrange("p (r o) -> p r o", o=1), cache[:, :, ds(f, 1)]).then_inc(up_r, 1)
                    dve.wait_ge(c0_r, l * (2 * NF) + q + 1)
                    dve.scalar_tensor_tensor(cv[:, :], upb[:, 1:1 + TC], convc[:, ds(f + 44, 1)], cv[:, :], ALU.mult, ALU.add).then_inc(up_seq, 1)
                    if adds is not None:
                        add_x(adds, 0, 0)
                    dve.wait_ge(up_seq, l * (2 * NF) + q + 1)
                    dve.scalar_tensor_tensor(cv[:, :], upb[:, 0:TC], convc[:, ds(f, 1)], cv[:, :], ALU.mult, ALU.add).then_inc(tap_r, 1)
                    if adds is not None:
                        add_x(adds + 1, 1, 1)
                    if slot is not None:
                        dve.wait_ge(tap_r, l * (2 * NF) + q + 1)
                        dve.wait_ge(gelu_r, l * NF + half(q - 1) + 1)
                        dve.tensor_tensor(cv[:, :], cv[:, :], cu[:, :], ALU.mult).then_inc(gmul_r, 1)
                        if adds is not None:
                            add_x(adds + 2, 2, 0)
                        dve.wait_ge(g_h, l * NF + half(q - 1) + 1)
                        dve.tensor_tensor(gHL[:, slot, 1], cv[:, :], gHL[:, slot, 0].bitcast(F32), ALU.subtract).then_inc(g_l, 1)

                for r, (f, slot) in enumerate(((0, None), (NF, 0), (1, None), (NF + 1, 2))):
                    up_tile(r, f, KT + r, r % 2, slot)
                    split_w(14 + r, 2 + r, (2 + r) % 3)

                def group(n, par, ahead):
                    s, u = n * 6 + 18, n * 12 + 12
                    up_tile(n * 4 + 4, n * 2 + 2, u, 0, None)
                    split_w(s, 0, 0)
                    up_tile(n * 4 + 5, n * 2 + 2 + NF, u + 1, 1, 1 - par, u + 2)
                    split_w(s + 1, 1, 1)
                    for m in range(3, KT):
                        add_x(u + 2 + m, m, m % 2)
                    if ahead:
                        split_w(s + 2, 2, 2)
                        split_w(s + 3, 3, 0)
                    up_tile(n * 4 + 6, n * 2 + 3, u + 10, 0, None)
                    if ahead:
                        split_w(s + 4, 4, 1)
                    up_tile(n * 4 + 7, n * 2 + 3 + NF, u + 11, 1, 2)
                    if ahead:
                        split_w(s + 5, 5, 2)

                with dve.Fori(0, (NG - 3) // 2) as j:
                    group(j * 2, 0, True)
                    group(j * 2 + 1, 1, True)
                group(NG - 3, 0, True)
                group(NG - 2, 1, False)
                for m in range(KT):
                    add_x(N_USE - KT + m, m, m % 2)
                    if m:
                        if m > 1:
                            add_square(dve, l * 2 + 2, m - 1)
                        low_part(dve, l * 2 + 2, m - 1)
                add_square(dve, l * 2 + 2, KT - 1)
                low_part(dve, l * 2 + 2, KT - 1)
                mean_square(dve, l * 2 + 2)
                dve.wait_ge(bank_free, M0 + 3 * N_USE)
                dve.memset(convc[:, 0:1], 0.0).then_inc(x_done, 1)

            dve.wait_ge(rt_r, 2 * DEPTH + 1)
            for i, (t0, r) in enumerate(TOK):
                dve.wait_ge(y_tp, i + 1)
                wait(dve, (y_st0, y_st1)[i % 2], 16 * (i // 2))
                dve.tensor_scalar(yst[0:r, i % 2, 512:1024], bank[2 * (i % 2) + 1][0:r, :], rt[0:r, i:i + 1], None,
                                  ALU.mult).then_inc(y_ev, 1)


LINKS, LINKS_SAMPLE = 24, 20

RAW_AT, RAW_PER = {}, [0, 0, 0]
for _s in range(18):
    RAW_PER[_s % 3] += 64 if _s < KT else 16
    RAW_AT[_s] = RAW_PER[_s % 3]
RAW_12 = [RAW_AT[9], RAW_AT[10], RAW_AT[11]]
RAW_PER = [RAW_12[0] + 20 * 16 + 16, RAW_12[1] + 20 * 16 + 16, RAW_12[2] + 20 * 16]


def half(q):
    return q // 2 if isinstance(q, int) else q // 2


_INS = ["x_prompt", "x_sample", "cache_k", "cache_v", "state_C", "state_n", "state_m", "cache_conv", "attn_norm",
        "w_in", "gmlp_norm", "gmlp_w", "gmlp_b", "attn_sinks", "mlstm_gate_b", "w_out", "ffn_norm", "w_up",
        "conv_w", "conv_b", "w_down", "final_norm"]
_OUTS = [("y_prompt", (1, SEQ, D)), ("y_sample", (1, DEC, D)),
         ("prompt_k", (DEPTH, 1, P, 2, HD)), ("prompt_v", (DEPTH, 1, P, 2, HD)),
         ("prompt_C", (DEPTH, 1, 4, HD, HD)), ("prompt_n", (DEPTH, 1, 4, HD)), ("prompt_m", (DEPTH, 1, 4)),
         ("prompt_conv", (DEPTH, 1, 2, 2 * FF)),
         ("sample_gmlp_v", (DEPTH, 1, DEC, 256)), ("sample_k", (DEPTH, 1, DEC, 2, HD)), ("sample_v", (DEPTH, 1, DEC, 2, HD)),
         ("sample_C", (DEPTH, 1, 4, HD, HD)), ("sample_n", (DEPTH, 1, 4, HD)), ("sample_m", (DEPTH, 1, 4)),
         ("sample_conv", (DEPTH, 1, 2, 2 * FF))]


def kernel(**inputs):
    import concourse.bacc as bacc
    from concourse.bass_utils import run_bass_kernel_spmd

    nc = bacc.Bacc("TRN2", target_bir_lowering=False, num_devices=1)
    arrays = {f"in_{n}": np.ascontiguousarray(inputs[n]) for n in _INS}
    arrays["in_consts"] = constants()
    I = {n[3:]: nc.dram_tensor(n, a.shape, mybir.dt.from_np(a.dtype), kind="ExternalInput").ap() for n, a in arrays.items()}
    O = {n: nc.dram_tensor(f"out_{n}", s, F32, kind="ExternalOutput").ap() for n, s in _OUTS}
    build(nc, I, O)
    r = run_bass_kernel_spmd(nc, [arrays], core_ids=[0])
    return tuple(r.results[0][f"out_{n}"] for n, _ in _OUTS)
```

```python
from contextlib import ExitStack

import numpy as np

import concourse.bass as bass
from concourse import mybir

F32 = mybir.dt.float32
F32R = mybir.dt.float32r
ALU = mybir.AluOpType
ACT = mybir.ActivationFunctionType
AX = mybir.AxisListType
ds = bass.ds

P = 128
D = 1024
KT = D // P
SEQ = 1024
DEPTH = 2
DEC = 64
PAST = 128
HD = 64
FF = 2816
NF = FF // P
PAD = 2
TC = SEQ + PAD + DEC
SOFF = SEQ + PAD
CH = [(0, 364), (364, 364), (728, 362)]
NB = SEQ // P
TOK = [(i * P, P) for i in range(NB)] + [(SOFF, DEC)]
NTOK = len(TOK)
ZW = 2312
A_U, A_V, B_Q, B_K, B_V, C_Q, C_K, C_V, C_O, C_G = 0, 256, 512, 1024, 1152, 1280, 1536, 1792, 2048, 2304
ZA, ZB = 512, 450
SCALE = HD ** -0.5
EPS = 1e-6
BIG = 1e30
ROT = 16
THETA = 500000.0

CI, CU, CM, CCOS, CSIN = 0, P, 2 * P, 3 * P, 3 * P + NTOK * ROT
CW = 3 * P + 2 * NTOK * ROT


def constants():
    t = np.zeros((P, CW), np.float32)
    t[:, CI:CI + P] = np.eye(P)
    t[:, CU:CU + P] = np.triu(np.ones((P, P)))
    t[:, CM:CM + P] = np.where(np.tril(np.ones((P, P))) > 0, 0.0, -BIG)
    half = ROT // 2
    inv = (np.float32(THETA) ** (-np.arange(half, dtype=np.float32) / np.float32(half))).astype(np.float32)
    for i in range(NTOK):
        pos = (np.arange(P) + (i * P if i < NB else PAST)).astype(np.float32)
        ang = (pos[:, None] * inv[None, :]).astype(np.float32)
        c, s = np.cos(ang), np.sin(ang)
        t[:, CCOS + i * ROT:CCOS + (i + 1) * ROT] = np.concatenate([c, c], 1)
        t[:, CSIN + i * ROT:CSIN + (i + 1) * ROT] = np.concatenate([-s, s], 1)
    return t


def wait(eng, sem, value):
    if isinstance(value, int) and value <= 0:
        return
    eng.wait_ge(sem, value)


def settle(eng, settled):
    eng.sem_inc(settled, 1)


class Chain:

    def __init__(self, eng, sem, base):
        self.eng, self.sem, self.base, self.n = eng, sem, base, 0

    def link(self, ins):
        self.n += 1
        ins.then_inc(self.sem, 1)
        self.eng.wait_ge(self.sem, self.base + self.n)


def build(nc, I, O):
    ctx = ExitStack()

    def sem(name):
        return ctx.enter_context(nc.semaphore(name))

    def sb(name, shape, dt=F32, c=ctx):
        return c.enter_context(nc.sbuf_tensor(name, shape, dt))

    with ctx:
        bank = [ctx.enter_context(nc.psum_tensor(f"bank{i}", [P, 512], F32)) for i in range(8)]
        z_dram = nc.dram_tensor("z_scratch", (NTOK * P, ZW), F32, kind="Internal").ap()

        xT = sb("xT", [P, KT, TC])
        actH = sb("actH", [P, KT, TC], F32R)
        actL = sb("actL", [P, KT, TC], F32R)
        ident = sb("ident", [P, P])
        ones = sb("ones", [P, P])
        gains = sb("gains", [P, (2 * DEPTH + 1) * KT])
        rstd_cu = sb("rstd_cu", [P, 2, TC])
        rstd = rstd_cu[:, 0]
        cu = rstd_cu[:, 1]
        upb = sb("upb", [P, PAD + TC])
        convc = sb("convc", [P, 264])
        convst = sb("convst", [P, 4, 2 * NF])
        stat = sb("stat", [P, 3 * NTOK])
        rt = stat[:, 0:NTOK]
        ms = stat[:, NTOK:2 * NTOK]
        mhalf = stat[:, 2 * NTOK:3 * NTOK]

        with ExitStack() as c:
            rawz = sb("rawz", [P, KT, ZA], c=c)
            wzH1, wzL1 = (sb(n, [P, KT, ZB], F32R, c=c) for n in ("wzH1", "wzL1"))
            wzH0, wzL0 = (sb(n, [P, KT, ZA], F32R, c=c) for n in ("wzH0", "wzL0"))
            wzH, wzL = [wzH0, wzH1], [wzL0, wzL1]
            zst = sb("zst", [P, 3, ZA], c=c)
            identr = sb("identr", [P, P], F32R, c=c)
            grows = sb("grows", [(2 * DEPTH + 1) * KT, P], c=c)
            xin = yst = rawz[:, 0:4].rearrange("p (b a) n -> p b (a n)", b=2)
        with ExitStack() as c:
            table = sb("table", [P, CW], c=c)
            rows = sb("rows", [88, 3, P], c=c)
            gw = sb("gw", [P, 4, P], c=c)
            gwT = sb("gwT", [P, 4, P], c=c)
            gbias = sb("gbias", [P, 2, P], c=c)
            ggain = sb("ggain", [P, 256], c=c)
            sink = sb("sink", [P, 4], c=c)
            nsink = sb("nsink", [P, 4], c=c)
            gateb = sb("gateb", [P, 8], c=c)
            ckin = sb("ckin", [P, P], c=c)
            stin = sb("stin", [HD + 1, 256], c=c)
            CN = [sb(f"CN{i}", [P, 2, HD + 1], c=c) for i in range(2)]
            mp = [sb(f"mp{i}", [P, 4], c=c) for i in range(2)]
            vprev = [sb(f"vprev{i}", [P, P], c=c) for i in range(2)]
            kTw = sb("kTw", [P, 2 * P], c=c)
            qz = sb("qz", [P, 4, P], c=c)
            Vx = sb("Vx", [P, 4, HD + 1], c=c)
            prob = [sb(f"prob{i}", [P, 4, 2 * P], c=c) for i in range(2)]
            zb0 = sb("zb0", [P, ZW], c=c)
            qp = sb("qp", [P, 512], c=c)
            rp1 = sb("rp1", [P, 10, ROT], c=c)
            rp2 = sb("rp2", [P, 10, ROT], c=c)
            zb = [zb0, sb("zb1", [P, ZW], c=c)]
            bqT = sb("bqT", [P, 4, P], c=c)
            pT = [sb(f"pT{i}", [P, 2, 4, P], c=c) for i in range(2)]
            mx = sb("mx", [P, 2, 4], c=c)
            nm = sb("nm", [P, 2, 4], c=c)
            es = sb("es", [P, 2, 4], c=c)
            rs = sb("rs", [P, 2, 4], c=c)
            uT = sb("uT", [P, 2, P], c=c)
            vsq = sb("vsq", [P, 256], c=c)
            vss = sb("vss", [P, 1], c=c)
            rv = sb("rv", [P, 1], c=c)
            vn = sb("vn", [P, 256], c=c)
            mixA = sb("mixA", [P, 2, P], c=c)
            ckT = sb("ckT", [P, 2, P], c=c)
            g8 = sb("g8", [P, 8], c=c)
            ax = sb("ax", [P, 4], c=c)
            lf = sb("lf", [P, 4], c=c)
            bb = sb("bb", [P, 8], c=c)
            aa = sb("aa", [P, 4], c=c)
            dA = sb("dA", [P, 4 * P], c=c)
            Am = sb("Am", [P, 4, P], c=c)
            cm = sb("cm", [P, 4], c=c)
            G = sb("G", [P, 4], c=c)
            sm = sb("sm", [P, 16], c=c)
            ex = sb("ex", [P, 16], c=c)
            exk = sb("exk", [P, 4], c=c)
            Wt = sb("Wt", [P, 4, P], c=c)
            WTs = sb("WTs", [P, 4, P], c=c)
            kw = sb("kw", [P, 256], c=c)
            nd = sb("nd", [P, 4, HD + 1], c=c)
            dn = sb("dn", [P, 4], c=c)
            eo = sb("eo", [P, 256], c=c)
            hc = sb("hc", [P, 256], c=c)
            dec = sb("dec", [P, 2], c=c)
            stout = sb("stout", [HD + 1, 4, P], c=c)
        with ExitStack() as c:
            wH = sb("wH", [P, 6, KT, P], F32R, c=c)
            wL = sb("wL", [P, 6, KT, P], F32R, c=c)
            raw = sb("raw", [P, 3, KT, P], c=c)
            gHL = sb("gHL", [P, 3, 2, TC], F32R, c=c)
            cv = sb("cv", [P, TC], c=c)
            cvo = cv[0:88, 0:2 * P].rearrange("p (s n) -> p s n", s=2)
        with ExitStack() as c:
            c.enter_context(nc.sbuf_tensor("weights_place", [P, 15 * KT * P * 4], mybir.dt.uint8))
            diag = sb("diag", [P, NTOK, P], c=c)

        settled = sem("settled")
        const_in, s_ones, xin_in0, xin_in1, xin_tp, xin_ea, xin_ev, x_done = map(sem, (
            "const_in", "s_ones", "xin_in0", "xin_in1", "xin_tp", "xin_ea", "xin_ev", "x_done"))
        rows_in, rows_tp, gains_r, conv_r = map(sem, ("rows_in", "rows_tp", "gains_r", "conv_r"))
        sq_r, acc_r, act_h, act_l, ssq_mm, ms_r, rt_r = map(sem, (
            "sq_r", "acc_r", "act_h", "act_l", "ssq_mm", "ms_r", "rt_r"))
        rz_in, wz_h, wz_l, z_mm, z_ev = map(sem, ("rz_in", "wz_h", "wz_l", "z_mm", "z_ev"))
        z_st = [sem(f"z_st{i}") for i in range(3)]
        par_in, z_in0, z_in1, par_tp, gwT_r, ck_r, cn_r, init_r, v_init = map(sem, (
            "par_in", "z_in0", "z_in1", "par_tp", "gwT_r", "ck_r", "cn_r", "init_r", "v_init"))
        z_in = [z_in0, z_in1]
        MIX = ("rope_r qp_r tC_r tU_r tB_r ax_r ax_e lg_r lf_r cum_r bb_r aa_r dA_r A_r A_used sm_r ex_r exk_r D_r P_r "
               "qk_r W_r WT_r WTs_r vss_r vms_r rv_r vn_r bq_r kT_r cT_r mix_r mA_r int_r num_r hc_r hT_r eo_e eo_l eo_r "
               "kw_r kwmm_r cn_up pv_r hA_r hB_r hC_r vx_r keepk_r keepv_r blk_done").split()
        S = {n: sem(n) for n in MIX}
        S2 = {n: [sem(f"{n}{i}") for i in range(2)] for n in ("S_r", "nm_r", "e_r", "p_r", "PT_r", "pTa_r", "pTv_r")}
        kv_st, gv_st, sto_r, stt_r, st_st, mix_seq = map(sem, (
            "kv_st", "gv_st", "sto_r", "stt_r", "st_st", "mix_seq"))
        raw_in = [sem(f"raw_in{i}") for i in range(3)]
        w_h, w_l, mm, bank_free, w_used, diag_r, rs_mm, rstd_r = map(sem, (
            "w_h", "w_l", "mm", "bank_free", "w_used", "diag_r", "rs_mm", "rstd_r"))
        up_r, c0_r, tap_r, gelu_r, gmul_r, g_h, g_l, cvs_r, cvt_r, cvo_r, cvo_st, up_seq, rp_r = map(sem, (
            "up_r", "c0_r", "tap_r", "gelu_r", "gmul_r", "g_h", "g_l", "cvs_r", "cvt_r", "cvo_r", "cvo_st", "up_seq", "rp_r"))
        y_tp, y_ea, y_ev, y_st0, y_st1, identr_r = map(sem, ("y_tp", "y_ea", "y_ev", "y_st0", "y_st1", "identr_r"))

        N_W = KT + 3 * NF
        N_USE = KT + 2 * NF + KT * (NF // 2)
        NG = NF // 2

        def split3(pe, out, aH, aL, bH, bL, first, last):
            pe.matmul(out, aH, bH, start=first, stop=False)
            pe.matmul(out, aH, bL, start=False, stop=False)
            return pe.matmul(out, aL, bH, start=False, stop=last)

        def square(act, n, k):
            if k >= 3:
                act.wait_ge(acc_r, n * (KT - 1) + k - 2)
            dst = rstd[:, :] if k == 0 else (upb[:, 0:TC] if k % 2 else cu[:, :])
            act.activation(dst, xT[:, k], ACT.Square).then_inc(sq_r, 1)

        def high_part(act, n, k):
            act.activation(actH[:, k], xT[:, k], ACT.Copy, scale=gains[:, ds(n * KT + k, 1)]).then_inc(act_h, 1)

        def add_square(dve, n, k):
            dve.wait_ge(sq_r, n * KT + k + 1)
            if k >= 2:
                dve.wait_ge(acc_r, n * (KT - 1) + k - 1)
            sq = upb[:, 0:TC] if k % 2 else cu[:, :]
            dve.tensor_tensor(rstd[:, :], rstd[:, :], sq, ALU.add).then_inc(acc_r, 1)

        def low_part(dve, n, k):
            dve.wait_ge(act_h, n * KT + k + 1)
            dve.scalar_tensor_tensor(actL[:, k], xT[:, k], gains[:, ds(n * KT + k, 1)],
                                     actH[:, k].bitcast(F32), ALU.mult, ALU.subtract).then_inc(act_l, 1)

        def mean_square(dve, n):
            dve.wait_ge(ssq_mm, n + 1)
            dve.tensor_scalar(ms[:, 0:NB], bank[6][:, 0:NB], 1.0 / D, EPS, ALU.mult, ALU.add).then_inc(ms_r, 1)
            dve.tensor_scalar(ms[0:DEC, NB:NB + 1], bank[6][0:DEC, NB:NB + 1], 1.0 / D, EPS,
                              ALU.mult, ALU.add).then_inc(ms_r, 1)

        def norm_pe(pe, n):
            pe.wait_ge(acc_r, (n + 1) * (KT - 1))
            for i, (t0, r) in enumerate(TOK):
                m = pe.matmul(bank[6][0:r, i:i + 1], rstd[:, t0:t0 + r], ones[:, 0:1], start=True, stop=True)
            m.then_inc(ssq_mm, 1)

        def norm_pool(pool, n):
            pool.wait_ge(ms_r, 2 * n + 2)
            pool.tensor_tensor(rt[:, :], ms[:, :], mhalf[:, :], ALU.pow).then_inc(rt_r, 1)

        def each_block(body, eng):
            first, second = (0, 0, 0, P, "first"), (1, 1, 0, P, "mid")
            last, sample = (1, 7, 3, P, "last"), (0, 8, 4, DEC, "sample")
            body(None, first)
            body(first, second)
            with eng.Fori(0, 3) as j:
                odd, even, odd2 = (1, j * 2 + 1, j, P, "mid"), (0, j * 2 + 2, j + 1, P, "mid"), (1, j * 2 + 3, j + 1, P, "mid")
                body(odd, even)
                body(even, odd2)
            body(last, sample)
            body(sample, None)

        Z_LOADS = (5, 4)

        def cols(i, r):
            return slice(SOFF, SOFF + DEC) if r == DEC else ds(i * P, P)

        block = ctx.enter_context(nc.Block())

        @block.sync
        def _(sp):
            sp.dma_start(ident[:, :], I["consts"][:, CI:CI + P]).then_inc(const_in, 16)

            for n, (name, l) in enumerate([(f"{part}_norm", l) for l in range(DEPTH) for part in ("attn", "ffn")]):
                sp.dma_start(grows[n * KT:(n + 1) * KT, :], I[name][l].rearrange("(a b) -> a b", b=P)).then_inc(rows_in, 16)
            sp.dma_start(grows[2 * DEPTH * KT:, :], I["final_norm"].rearrange("(a b) -> a b", b=P)).then_inc(rows_in, 16)

            def load_x(par, t, src, r):
                wait(sp, xin_tp, t - 1)
                sp.dma_start(xin[0:r, par], src).then_inc((xin_in0, xin_in1)[par], 16)

            xp = I["x_prompt"][0].rearrange("(i p) d -> i p d", p=P)
            load_x(0, 0, xp[0], P)
            load_x(1, 1, xp[1], P)
            with sp.Fori(1, 4) as j:
                load_x(0, j * 2, xp[ds(j * 2, 1)].rearrange("o p d -> (o p) d"), P)
                load_x(1, j * 2 + 1, xp[ds(j * 2 + 1, 1)].rearrange("o p d -> (o p) d"), P)
            load_x(0, 8, I["x_sample"][0], DEC)

            with sp.Fori(0, DEPTH) as l:
                sp.wait_ge(x_done, l + 1)
                w_in = I["w_in"][l].rearrange("(k p) n -> p k n", p=P)

                def load_wz(g, c0, w):
                    sp.wait_ge(wz_l, l * 5 + g)
                    sp.dma_start(rawz[:, :, 0:w], w_in[:, :, ds(c0, w)]).then_inc(rz_in, 16)

                def load_mixers():
                    sp.wait_ge(wz_l, l * 5 + 5)
                    settle(sp, settled)
                    sp.wait_ge(z_mm, l * 45 + 36)
                    settle(sp, settled)
                    sp.dma_start(table[:, :], I["consts"]).then_inc(par_in, 16)
                    for name, i0, s in (("conv_w", 0, 0), ("conv_w", 1, 0), ("conv_w", 2, 1)):
                        sp.dma_start(rows[44 * (i0 % 2):44 * (i0 % 2) + 44, s],
                                     I[name][l, i0].rearrange("(a b) -> a b", b=P)).then_inc(par_in, 16)
                    sp.dma_start(rows[44:88, 1], I["conv_b"][l].rearrange("(a b) -> a b", b=P)).then_inc(par_in, 16)
                    for i0 in range(2):
                        sp.dma_start(rows[44 * i0:44 * i0 + 44, 2],
                                     I["cache_conv"][l, 0, i0].rearrange("(a b) -> a b", b=P)).then_inc(par_in, 16)
                    sp.dma_start(gw[:, :, :], I["gmlp_w"][l].rearrange("h i j -> i h j")).then_inc(par_in, 16)
                    for h in range(4):
                        sp.dma_start(gbias[64 * (h % 2):64 * (h % 2) + 64, h // 2],
                                     I["gmlp_b"][l, h:h + 1, :].broadcast_to([64, P])).then_inc(par_in, 16)
                    sp.dma_start(ggain[:, :], I["gmlp_norm"][ds(l, 1), :].broadcast_to([P, 256])).then_inc(par_in, 16)
                    for h in range(2):
                        sp.dma_start(sink[64 * h:64 * h + 64, :],
                                     I["attn_sinks"][ds(l, 1), 4 * h:4 * h + 4].broadcast_to([64, 4])).then_inc(par_in, 16)
                    sp.dma_start(gateb[:, :], I["mlstm_gate_b"][ds(l, 1), :].broadcast_to([P, 8])).then_inc(par_in, 16)
                    sp.dma_start(mp[1][:, :], I["state_m"][l, 0:1, :].broadcast_to([P, 4])).then_inc(par_in, 16)
                    sp.dma_start(vprev[1][:, :], I["cache_v"][l, 0].rearrange("t h d -> t (h d)")).then_inc(par_in, 16)
                    sp.dma_start(ckin[:, :], I["cache_k"][l, 0].rearrange("t h d -> t (h d)")).then_inc(par_in, 16)
                    sp.dma_start(stin[0:HD, :].rearrange("v (h k) -> v h k", k=HD),
                                 I["state_C"][l, 0].rearrange("h v k -> v h k")).then_inc(par_in, 16)
                    sp.dma_start(stin[HD:HD + 1, :], I["state_n"][l, 0:1].rearrange("o h k -> o (h k)")).then_inc(par_in, 16)
                    sp.wait_ge(z_st[0], (l * 15 + 13) * 16)
                    settle(sp, settled)
                    sp.dma_start(zb[0][:, :], z_dram[0:P, :]).then_inc(z_in[0], 16)

                def store_z(g, c0, w):
                    for i, (t0, r) in enumerate(TOK):
                        sp.wait_ge(z_ev, l * 45 + g * 9 + i + 1)
                        sp.dma_start(z_dram[i * P:i * P + r, ds(c0, w)], zst[0:r, i % 3, 0:w]).then_inc(z_st[i % 3], 16)
                        if isinstance(g, int) and g == 4 and i == 2:
                            load_mixers()

                sp.dma_start(rawz[:, :, 0:ZA], w_in[:, :, 0:ZA]).then_inc(rz_in, 16)
                load_wz(1, ZA, ZB)
                store_z(0, 0, ZA)
                with sp.Fori(1, 4) as g:
                    load_wz(g + 1, g * ZB + ZA, ZB)
                    store_z(g, g * ZB + (ZA - ZB), ZB)
                store_z(4, 3 * ZB + ZA, ZB)

                def mixer(b, nx):
                    if nx is None:
                        return
                    par, i, zi, r, kind = nx
                    if b is not None:
                        before = b[1]
                        if kind == "mid" and isinstance(i, int):
                            for s in z_st:
                                sp.wait_ge(s, (l + 1) * 5 * 3 * 16)
                        else:
                            sp.wait_ge(S["blk_done"], l * 9 + before)
                    src = z_dram[NB * P:NB * P + DEC, :] if kind == "sample" else z_dram[ds(i * P, P), :]
                    if b is not None:
                        settle(sp, settled)
                        sp.dma_start(zb[par][0:r, :], src).then_inc(z_in[par], 16)

                each_block(mixer, sp)
                sp.wait_ge(S["blk_done"], l * 9 + 8)
                settle(sp, settled)
                for q, dst in ((B_K, "prompt_k"), (B_V, "prompt_v")):
                    sp.dma_start(O[dst][l, 0].rearrange("t h d -> t (h d)"), zb[1][:, q:q + P]).then_inc(kv_st, 16)
                sp.wait_ge(S["blk_done"], l * 9 + 9)
                settle(sp, settled)
                for q, dst in ((B_K, "sample_k"), (B_V, "sample_v")):
                    sp.dma_start(O[dst][l, 0].rearrange("t h d -> t (h d)"), zb[0][0:DEC, q:q + P]).then_inc(kv_st, 16)
                sp.dma_start(O["sample_gmlp_v"][l, 0], vn[0:DEC, :]).then_inc(gv_st, 16)
                sp.wait_ge(sto_r, l + 1)
                settle(sp, settled)
                for g, part in enumerate(("prompt", "sample")):
                    sp.dma_start(O[part + "_C"][l, 0].rearrange("h v k -> v h k"),
                                 stout[0:HD, 2 * g:2 * g + 2].rearrange("v a (h k) -> v (a h) k", k=HD)).then_inc(st_st, 16)
                    sp.dma_start(O[part + "_n"][l, 0:1].rearrange("o h k -> o (h k)"),
                                 stout[HD:HD + 1, 2 * g:2 * g + 2].rearrange("v a k -> v (a k)")).then_inc(st_st, 16)
                    sp.dma_start(O[part + "_m"][l, 0:1], mp[g][0:1, :]).then_inc(st_st, 16)
                sp.wait_ge(kv_st, l * 64 + 64)
                settle(sp, settled)
                sp.wait_ge(gv_st, l * 16 + 16)
                settle(sp, settled)
                sp.wait_ge(st_st, l * 96 + 96)
                settle(sp, settled)

                w_out, w_up, w_down = I["w_out"][l], I["w_up"][l].rearrange("(k p) n -> p k n", p=P), I["w_down"][l]

                def load_w(s, slot, parts):
                    if not (isinstance(s, int) and s < 3):
                        sp.wait_ge(w_l, l * N_W + s - 2)
                    for k, (dst, src) in enumerate(parts):
                        sp.dma_start(dst, src).then_inc(raw_in[slot], 16)

                for m in range(KT):
                    t = raw[:, m % 3]
                    c = slice(m * P, m * P + P)
                    load_w(m, m % 3, [
                        (t[:, 0:2], w_out[0:256, c].rearrange("(k p) n -> p k n", p=P)),
                        (t[0:64, 2:6], w_out[256:512, c].rearrange("(k p) n -> p k n", p=64)),
                        (t[64:128, 2:6], w_out[512:768, c].rearrange("(k p) n -> p k n", p=64)),
                        (t[:, 6:8], w_out[768:1024, c].rearrange("(k p) n -> p k n", p=P))])

                def load_up(s, slot, f):
                    load_w(s, slot, [(raw[:, slot], w_up[:, :, ds(f * P, P)])])

                def load_down(s, slot, f):
                    load_w(s, slot, [(raw[:, slot].rearrange("p k n -> p (k n)"), w_down[ds(f * P, P), :])])

                for r, f in enumerate((0, NF, 1, NF + 1)):
                    load_up(KT + r, (KT + r) % 3, f)
                with sp.Fori(0, NG - 1) as n:
                    s = n * 6 + 12
                    load_up(s, 0, n * 2 + 2)
                    load_up(s + 1, 1, n * 2 + 2 + NF)
                    load_down(s + 2, 2, n * 2)
                    load_down(s + 3, 0, n * 2 + 1)
                    load_up(s + 4, 1, n * 2 + 3)
                    load_up(s + 5, 2, n * 2 + 3 + NF)
                load_down(N_W - 2, 0, NF - 2)
                load_down(N_W - 1, 1, NF - 1)

                sp.wait_ge(cvo_r, l + 1)
                for s, dst in ((0, "prompt_conv"), (1, "sample_conv")):
                    sp.dma_start(O[dst][l, 0].rearrange("r (a b) -> (r a) b", b=P), cvo[:, s]).then_inc(cvo_st, 16)
                sp.wait_ge(cvo_st, l * 32 + 32)
                settle(sp, settled)

            for i in range(NTOK):
                sp.wait_ge(y_ea, i + 1)
                sp.wait_ge(y_ev, i + 1)
                dst = O["y_sample"][0] if i == NB else O["y_prompt"][0, i * P:(i + 1) * P, :]
                sp.dma_start(dst, yst[0:TOK[i][1], i % 2]).then_inc((y_st0, y_st1)[i % 2], 16)
            sp.wait_ge(y_st0, 80)
            sp.wait_ge(y_st1, 64)

        @block.tensor
        def _(pe):
            pe.wait_ge(const_in, 16)

            def turn_x(par, t, n, r):
                pe.wait_ge((xin_in0, xin_in1)[par], n * 16)
                wait(pe, xin_ea, t - 1)
                wait(pe, xin_ev, t - 1)
                for k in range(KT):
                    m = pe.transpose(bank[2 * par + k // 4][:, (k % 4) * P:(k % 4) * P + r],
                                     xin[0:r, par, k * P:(k + 1) * P], ident[0:r, 0:r])
                m.then_inc(xin_tp, 1)

            turn_x(0, 0, 1, P)
            turn_x(1, 1, 1, P)
            with pe.Fori(1, 4) as j:
                turn_x(0, j * 2, j + 1, P)
                turn_x(1, j * 2 + 1, j + 1, P)
            turn_x(0, 8, 5, DEC)
            n = (2 * DEPTH + 1) * KT
            pe.wait_ge(rows_in, (2 * DEPTH + 1) * 16)
            pe.transpose(bank[7][:, 0:n], grows[0:n, :], ident[0:n, 0:n]).then_inc(rows_tp, 1)
            pe.wait_ge(s_ones, 3)
            norm_pe(pe, 0)

            with pe.Fori(0, DEPTH) as l:
                pe.wait_ge(x_done, l + 1)

                def z_group(g, par, w, u0):
                    pe.wait_ge(wz_l, l * 5 + g + 1)
                    for i, (t0, r) in enumerate(TOK):
                        if not (isinstance(g, int) and g == 0 and i < 6):
                            pe.wait_ge(z_ev, l * 45 + g * 9 + i - 5)
                        out = bank[(u0 + i) % 6][0:r, 0:w]
                        for k in range(KT):
                            if isinstance(g, int) and g == 0 and i == 0:
                                pe.wait_ge(act_l, l * (2 * KT) + k + 1)
                            m = split3(pe, out, actH[:, k, t0:t0 + r], actL[:, k, t0:t0 + r],
                                       wzH[par][:, k, 0:w], wzL[par][:, k, 0:w], k == 0, k == KT - 1)
                        m.then_inc(z_mm, 1)

                z_group(0, 0, ZA, 0)
                with pe.Fori(0, 2) as h:
                    z_group(h * 2 + 1, 1, ZB, 3)
                    z_group(h * 2 + 2, 0, ZB, 0)

                pe.wait_ge(par_in, (l + 1) * 336)
                for h in range(4):
                    m = pe.transpose(bank[6][:, h * P:(h + 1) * P], gw[:, h], ident[:, :])
                m.then_inc(par_tp, 1)
                for s in range(3):
                    m = pe.transpose(bank[7][:, s * 88:s * 88 + 88], rows[:, s], ident[0:88, 0:88])
                m.then_inc(par_tp, 1)
                pe.wait_ge(z_ev, l * 45 + 45)
                pe.wait_ge(init_r, l * INIT + INIT)

                def small(r):
                    if r == DEC:
                        settle(pe, settled)

                def front_a(nx):
                    par, i, zi, r, kind = nx
                    b1 = l * 9 + i + 1
                    z = zb[par]
                    pe.wait_ge(z_in[par], (l * Z_LOADS[par] + zi + 1) * 16)
                    small(r)
                    for s in range(4):
                        m = pe.transpose(bank[0][:, s * P:s * P + r], z[0:r, C_Q + s * P:C_Q + (s + 1) * P], ident[0:r, 0:r])
                    m.then_inc(S["tC_r"], 1)
                    pe.wait_ge(S["qp_r"], b1)
                    small(r)
                    for s in range(4):
                        m = pe.transpose(bank[1][:, s * P:s * P + r], qp[0:r, s * P:(s + 1) * P], ident[0:r, 0:r])
                    m.then_inc(S["tB_r"], 1)

                def front_b(nx):
                    par, i, zi, r, kind = nx
                    b1 = l * 9 + i + 1
                    z = zb[par]
                    for s in range(2):
                        pe.transpose(bank[2][:, s * P:s * P + r], z[0:r, A_U + s * P:A_U + (s + 1) * P], ident[0:r, 0:r])
                    pe.wait_ge(S["rope_r"], b1)
                    small(r)
                    pe.transpose(bank[2][:, 2 * P:2 * P + r], z[0:r, B_K:B_K + P], ident[0:r, 0:r]).then_inc(S["tU_r"], 1)
                    if kind == "sample":
                        pe.transpose(bank[3][:, P:2 * P], ckin[:, :], ident[:, :])
                        for s in range(2):
                            pe.transpose(bank[3][:, 2 * P + s * 65:2 * P + s * 65 + 65], stin[:, s * P:(s + 1) * P], ident[0:65, 0:65])
                    pe.wait_ge(S["lf_r"], b1)
                    small(r)
                    pe.matmul(bank[3][0:r, 0:4], table[0:r, CU:CU + r], lf[0:r, :], start=True, stop=True)
                    pe.matmul(bank[3][:, 4:8], ones[0:r, :], lf[0:r, :], start=True, stop=True).then_inc(S["cum_r"], 1)

                def scores(nx):
                    par, i, zi, r, kind = nx
                    b1 = l * 9 + i + 1
                    pe.wait_ge(S["bq_r"], b1)
                    pe.wait_ge(S["cT_r"], b1)
                    pe.wait_ge(S["kT_r"], b1)
                    if kind == "sample":
                        pe.wait_ge(cn_r, l * 2 + 2)
                    settle(pe, settled)
                    for c in range(1 if kind == "sample" else 2):
                        k0, k1 = (128 if kind == "first" else 64 * c), 192 + 64 * c
                        if c:
                            pe.wait_ge(S["bb_r"], b1)
                            settle(pe, settled)
                        for p in range(4):
                            for v in range(2):
                                m = pe.matmul(bank[2 * c + p // 2][64 * v:64 * v + 64, (p % 2) * 256 + k0:(p % 2) * 256 + k1],
                                              bqT[64 * v:64 * v + 64, p, 64 * c:64 * c + 64],
                                              kTw[64 * v:64 * v + 64, k0:k1], start=True, stop=True)
                        m.then_inc(S2["S_r"][c], 1)

                def back(b, nx):
                    par, i, zi, r, kind = b
                    b1 = l * 9 + i + 1
                    c1 = l * 8 + i + 1
                    z = zb[par]
                    nch = 1 if kind == "sample" else 2
                    g = 1 if kind == "sample" else 0
                    if kind != "first":
                        pe.wait_ge(S["cn_up"], b1 - 1)
                    small(r)
                    for h in range(4):
                        m = pe.matmul(bank[4][0:r, h * P:h * P + r], qz[:, h, 0:r], ckT[:, h // 2, 0:r],
                                      start=True, stop=True)
                    m.then_inc(S["qk_r"], 1)
                    pe.wait_ge(S["dA_r"], b1)
                    if kind == "first":
                        pe.wait_ge(gwT_r, l + 1)
                        pe.wait_ge(conv_r, l + 1)
                    small(r)
                    pe.matmul(bank[6][:, 0:4 * r], ones[0:r, :], dA[0:r, 0:4 * r], start=True, stop=True).then_inc(S["A_r"], 1)
                    if kind != "first":
                        pe.wait_ge(S["blk_done"], b1 - 1)
                    pe.wait_ge(S["vn_r"], b1)
                    small(r)
                    for h in range(4):
                        m = pe.matmul(bank[7][64 * (h % 2):64 * (h % 2) + 64, (h // 2) * P:(h // 2) * P + r],
                                      vn[0:r, h * 64:h * 64 + 64], gwT[0:r, h, 0:r], start=True, stop=True)
                    m.then_inc(S["mix_r"], 1)
                    for h in range(4):
                        m = pe.matmul(bank[5][0:r, h * 65:h * 65 + 65], qz[:, h, 0:r], CN[g][:, h // 2, :],
                                      start=True, stop=True)
                    m.then_inc(S["int_r"], 1)
                    for c in range(nch):
                        pe.wait_ge(S2["p_r"][c], b1 if c == 0 else c1)
                        for t in range(2):
                            for p in range(4):
                                m = pe.transpose(bank[2 * c + t][:, p * P:(p + 1) * P],
                                                 prob[c][:, p, t * P:(t + 1) * P], ident[:, :])
                        m.then_inc(S2["PT_r"][c], 1)
                    pe.wait_ge(S["W_r"], b1)
                    small(r)
                    for h in range(4):
                        m = pe.transpose(bank[4][0:r, h * P:h * P + r], Wt[0:r, h, 0:r], ident[0:r, 0:r])
                    m.then_inc(S["WT_r"], 1)
                    pe.wait_ge(S["mA_r"], b1)
                    for c in range(nch):
                        pe.wait_ge(S2["pTa_r"][c], b1 if c == 0 else c1)
                        pe.wait_ge(S2["pTv_r"][c], b1 if c == 0 else c1)
                        if c == 1:
                            front_a(nx)
                        for v in range(2):
                            for t in range(2):
                                n = DEC if (kind == "sample" and t == 1) else P
                                vt = z[0:n, B_V + 64 * v:B_V + 64 * v + 64] if t else vprev[g][:, 64 * v:64 * v + 64]
                                m = pe.matmul(bank[7][64 * v:64 * v + 64, 0:512].rearrange("d (p q) -> d p q", p=4)[:, :, 64 * c:64 * c + 64],
                                              vt, pT[c][0:n, t, :, 64 * v:64 * v + 64], start=(t == 0), stop=(t == 1))
                    m.then_inc(S["pv_r"], 1)
                    if nx is not None:
                        front_b(nx)
                    pe.wait_ge(S["WTs_r"], b1)
                    pe.wait_ge(S["vx_r"], b1)
                    pe.wait_ge(S["A_used"], b1)
                    small(r)
                    for h in range(4):
                        m = pe.matmul(bank[6][0:r, h * 65:h * 65 + 65], WTs[0:r, h, 0:r], Vx[0:r, h, :], start=True, stop=True)
                    m.then_inc(S["num_r"], 1)
                    pe.wait_ge(S["kw_r"], b1)
                    small(r)
                    for h in range(4):
                        m = pe.matmul(bank[4][64 * (h % 2):64 * (h % 2) + 64, (h // 2) * 65:(h // 2) * 65 + 65],
                                      kw[0:r, h * 64:h * 64 + 64], Vx[0:r, h, :], start=True, stop=True)
                    m.then_inc(S["kwmm_r"], 1)
                    if nx is not None:
                        scores(nx)
                    pe.wait_ge(S["hc_r"], b1)
                    small(r)
                    for s in range(2):
                        m = pe.transpose(bank[5][:, s * P:s * P + r], hc[0:r, s * P:(s + 1) * P], ident[0:r, 0:r])
                    m.then_inc(S["hT_r"], 1)

                def mixer(b, nx):
                    if b is None:
                        front_a(nx)
                        front_b(nx)
                        scores(nx)
                    else:
                        back(b, nx)

                each_block(mixer, pe)
                pe.wait_ge(S["blk_done"], l * 9 + 9)
                for g in range(2):
                    for s in range(2):
                        m = pe.transpose(bank[g][0:HD + 1, s * P:(s + 1) * P], CN[g][:, s, :], ident[:, :])
                m.then_inc(stt_r, 1)

                def set_use(u, s, c, w):
                    if not (isinstance(u, int) and u < 2):
                        pe.wait_ge(bank_free, l * (3 * N_USE) + (u - 2) * 3 + (c + 1))
                    return bank[3 * s + c][:, 0:w]

                def weights(s, slot, n=1):
                    pe.wait_ge(w_l, l * N_W + s + n)
                    return wH[:, slot], wL[:, slot]

                def product(u, uset, s, slot, fresh=False):
                    h, lo = weights(s, slot)
                    for c, (t0, w) in enumerate(CH):
                        out = set_use(u, uset, c, w)
                        for k in range(KT):
                            if fresh and c == 0:
                                pe.wait_ge(act_l, l * (2 * KT) + KT + k + 1)
                            m = split3(pe, out, h[:, k], lo[:, k], actH[:, k, t0:t0 + w], actL[:, k, t0:t0 + w],
                                       k == 0, k == KT - 1)
                        m.then_inc(mm, 1)

                pe.wait_ge(sto_r, l + 1)
                for m in range(KT):
                    product(m, m % 2, m, m % 6)
                norm_pe(pe, l * 2 + 1)
                product(KT, 0, KT, KT % 6, fresh=True)
                pe.wait_ge(diag_r, l + 1)
                pe.wait_ge(bank_free, l * (3 * N_USE) + 3 * KT)
                for s in range(3):
                    n = 3 if s < 2 else 2
                    m = pe.matmul(bank[3 + s][:, 0:n * P], ones[:, :], diag[:, 3 * s:3 * s + n], start=True, stop=True)
                m = pe.matmul(bank[5][:, 2 * P:2 * P + DEC], ones[0:DEC, :], diag[0:DEC, NB, 0:DEC], start=True, stop=True)
                m.then_inc(rs_mm, 1)
                pe.wait_ge(rstd_r, l * 5 + 5)
                for r in range(1, 4):
                    product(KT + r, r % 2, KT + r, (KT + r) % 6)

                def down(n, u, s, par):
                    pe.wait_ge(g_l, l * NF + n * 2 + 2)
                    weights(s, 2, 2)
                    for m in range(KT):
                        for c, (t0, w) in enumerate(CH):
                            out = set_use(u + m, m % 2, c, w)
                            for t, slot in enumerate((par, 2)):
                                h = wH[:, 2 + t].rearrange("p k n -> p (k n)")[:, m * P:(m + 1) * P]
                                lo = wL[:, 2 + t].rearrange("p k n -> p (k n)")[:, m * P:(m + 1) * P]
                                q = split3(pe, out, h, lo, gHL[:, slot, 0, t0:t0 + w], gHL[:, slot, 1, t0:t0 + w],
                                           t == 0, t == 1)
                            q.then_inc(mm, 1)

                def group(n, par):
                    s, u = n * 6 + 12, n * 12 + 12
                    product(u, 0, s, 0)
                    product(u + 1, 1, s + 1, 1)
                    down(n, u + 2, s + 2, par)
                    product(u + 10, 0, s + 4, 4)
                    product(u + 11, 1, s + 5, 5)

                with pe.Fori(0, (NG - 1) // 2) as j:
                    group(j * 2, 0)
                    group(j * 2 + 1, 1)
                pe.wait_ge(g_l, l * NF + NF)
                weights(N_W - 2, 0, 2)
                for m in range(KT):
                    for c, (t0, w) in enumerate(CH):
                        out = set_use(N_USE - KT + m, m % 2, c, w)
                        for t, slot in enumerate((0, 2)):
                            h = wH[:, t].rearrange("p k n -> p (k n)")[:, m * P:(m + 1) * P]
                            lo = wL[:, t].rearrange("p k n -> p (k n)")[:, m * P:(m + 1) * P]
                            q = split3(pe, out, h, lo, gHL[:, slot, 0, t0:t0 + w], gHL[:, slot, 1, t0:t0 + w],
                                       t == 0, t == 1)
                        q.then_inc(mm, 1)
                pe.wait_ge(cvs_r, (l + 1) * 4 * NF)
                for s in range(2):
                    m = pe.transpose(bank[7][0:88, s * P:(s + 1) * P],
                                     convst[:, 2 * s:2 * s + 2].rearrange("p r a -> p (r a)"), ident[:, :])
                m.then_inc(cvt_r, 1)
                norm_pe(pe, l * 2 + 2)

            pe.wait_ge(identr_r, 1)
            pe.wait_ge(act_l, (2 * DEPTH + 1) * KT)
            for i, (t0, r) in enumerate(TOK):
                wait(pe, y_ea, i - 1)
                wait(pe, y_ev, i - 1)
                for k in range(KT):
                    out = bank[2 * (i % 2) + k // 4][0:r, (k % 4) * P:(k % 4 + 1) * P]
                    pe.matmul(out, actH[:, k, t0:t0 + r], identr[:, :], start=True, stop=False)
                    m = pe.matmul(out, actL[:, k, t0:t0 + r], identr[:, :], start=False, stop=True)
                m.then_inc(y_tp, 1)

        @block.scalar
        def _(act):
            def turn_x(par, t, c0, r):
                act.wait_ge(xin_tp, t + 1)
                act.activation(xT[:, 0:4, c0], bank[2 * par][:, :].rearrange("p (k t) -> p k t", k=4)[:, :, 0:r],
                               ACT.Copy).then_inc(xin_ea, 1)

            turn_x(0, 0, ds(0, P), P)
            turn_x(1, 1, ds(P, P), P)
            with act.Fori(1, 4) as j:
                turn_x(0, j * 2, ds(j * 256, P), P)
                turn_x(1, j * 2 + 1, ds(j * 256 + P, P), P)
            turn_x(0, 8, slice(SOFF, TC), DEC)

            act.wait_ge(rows_tp, 1)
            act.activation(gains[:, :], bank[7][:, 0:(2 * DEPTH + 1) * KT], ACT.Copy).then_inc(gains_r, 1)
            act.wait_ge(gains_r, 1)
            act.wait_ge(x_done, 1)
            for k in range(KT):
                square(act, 0, k)
                high_part(act, 0, k)

            with act.Fori(0, DEPTH) as l:
                def split_wz(g, par, w):
                    act.wait_ge(rz_in, (l * 5 + g + 1) * 16)
                    if not (isinstance(g, int) and g < 2):
                        act.wait_ge(z_mm, l * 45 + (g - 1) * 9)
                    act.activation(wzH[par][:, :, 0:w], rawz[:, :, 0:w], ACT.Copy).then_inc(wz_h, 1)

                def evac_z(g, w, u0, func):
                    for i, (t0, r) in enumerate(TOK):
                        act.wait_ge(z_mm, l * 45 + g * 9 + i + 1)
                        if not (isinstance(g, int) and g == 0 and i < 3):
                            act.wait_ge(z_st[i % 3], (l * 15 + g * 3 + i // 3) * 16)
                        act.activation(zst[0:r, i % 3, 0:w], bank[(u0 + i) % 6][0:r, 0:w], func,
                                       scale=rt[0:r, i:i + 1]).then_inc(z_ev, 1)

                split_wz(0, 0, ZA)
                split_wz(1, 1, ZB)
                act.wait_ge(rt_r, l * 2 + 1)
                evac_z(0, ZA, 0, ACT.Gelu)
                for g in range(1, 5):
                    if g < 4:
                        split_wz(g + 1, (g + 1) % 2, ZB)
                    evac_z(g, ZB, 3 * (g % 2), ACT.Copy)

                act.preload_act_table_set("natural_log_exp_and_others")
                act.wait_ge(par_tp, l * 2 + 1)
                act.wait_ge(init_r, l * INIT + INIT)
                t = bank[6][:, :].rearrange("p (h i) -> p h i", h=4)
                act.activation(gwT[0:64], t[0:64], ACT.Copy)
                act.activation(gwT[64:128, :, 64:128], t[64:128, :, 64:128], ACT.Copy).then_inc(gwT_r, 1)
                act.wait_ge(par_tp, l * 2 + 2)
                act.activation(convc[:, :], bank[7][:, 0:264], ACT.Copy).then_inc(conv_r, 1)

                def front_early(nx):
                    par, i, zi, r, kind = nx
                    b1 = l * 9 + i + 1
                    z = zb[par]
                    act.wait_ge(z_in[par], (l * Z_LOADS[par] + zi + 1) * 16)
                    act.activation(vsq[0:r], z[0:r, A_V:A_V + 256], ACT.Square, accum_out=vss[0:r]).then_inc(S["vss_r"], 1)
                    act.wait_ge(S["rope_r"], b1)
                    act.activation(qp[0:r].rearrange("t (p v d) -> t p v d", p=4, v=2),
                                   z[0:r, B_Q:B_Q + 512].rearrange("t (v p d) -> t p v d", p=4, v=2), ACT.Copy).then_inc(S["qp_r"], 1)
                    act.wait_ge(S["ax_r"], b1)
                    act.activation(ax[0:r], ax[0:r], ACT.Exp, scale=-1.0).then_inc(S["ax_e"], 1)
                    act.wait_ge(S["ax_e"], b1)
                    act.activation(ax[0:r], ax[0:r], ACT.Ln, bias=1.0).then_inc(S["lg_r"], 1)

                def front_late(nx):
                    par, i, zi, r, kind = nx
                    b1 = l * 9 + i + 1
                    act.wait_ge(S["tC_r"], b1)
                    t = bank[0][:, :].rearrange("p (s t) -> p s t", s=4)
                    for v in range(2):
                        act.activation(qz[64 * v:64 * v + 64].rearrange("p (s v) t -> p s v t", v=2)[:, :, v, 0:r],
                                       t[64 * v:64 * v + 64, 0:2, 0:r], ACT.Copy)
                    act.activation(ckT[:, :, 0:r], t[:, 2:4, 0:r], ACT.Copy, scale=SCALE).then_inc(S["cT_r"], 1)
                    act.wait_ge(S["tU_r"], b1)
                    if kind == "mid":
                        act.wait_ge(S["keepk_r"], l * 7 + i)
                    t = bank[2][:, 0:3 * P].rearrange("p (s t) -> p s t", s=3)
                    act.activation(kTw[:, P:P + r], bank[2][:, 2 * P:2 * P + r], ACT.Copy)
                    act.activation(uT[:, :, 0:r], t[:, 0:2, 0:r], ACT.Copy).then_inc(S["kT_r"], 1)
                    if kind == "sample":
                        act.wait_ge(S["bb_r"], b1)
                        act.activation(kTw[:, 0:P], bank[3][:, P:2 * P], ACT.Copy).then_inc(cn_r, 1)
                        act.activation(CN[1][:, :, :], bank[3][:, 2 * P:2 * P + 130].rearrange("p (s k) -> p s k", s=2),
                                       ACT.Copy).then_inc(cn_r, 1)

                def back(b, nx):
                    par, i, zi, r, kind = b
                    b1 = l * 9 + i + 1
                    c1 = l * 8 + i + 1
                    z = zb[par]
                    nch = 1 if kind == "sample" else 2
                    act.activation(eo[0:r], z[0:r, C_O:C_O + 256], ACT.Exp, scale=-1.0).then_inc(S["eo_e"], 1)
                    act.wait_ge(S["eo_e"], b1)
                    act.activation(eo[0:r], eo[0:r], ACT.Ln, bias=1.0).then_inc(S["eo_l"], 1)
                    act.wait_ge(S["eo_l"], b1)
                    act.activation(eo[0:r], eo[0:r], ACT.Exp, scale=-1.0).then_inc(S["eo_r"], 1)
                    for c in range(nch):
                        k0, k1 = (128 if kind == "first" else 64 * c), 192 + 64 * c
                        act.wait_ge(S2["nm_r"][c], b1 if c == 0 else c1)
                        for p in range(4):
                            act.activation(prob[c][:, p, k0:k1], bank[2 * c + p // 2][:, (p % 2) * 256 + k0:(p % 2) * 256 + k1],
                                           ACT.Exp, bias=nm[:, c, p:p + 1], scale=SCALE, accum_out=rs[:, c, p:p + 1])
                        act.activation(es[:, c], es[:, c], ACT.Exp).then_inc(S2["e_r"][c], 1)
                    act.wait_ge(S["sm_r"], b1)
                    act.activation(ex[:, :], sm[:, :], ACT.Exp).then_inc(S["ex_r"], 1)
                    act.wait_ge(S["D_r"], b1)
                    act.activation(Am[0:r, :, 0:r], Am[0:r, :, 0:r], ACT.Exp).then_inc(S["P_r"], 1)
                    if nx is not None:
                        front_early(nx)
                    for c in range(nch):
                        act.wait_ge(S2["PT_r"][c], b1 if c == 0 else c1)
                        act.activation(pT[c][:, 1], bank[2 * c + 1][:, :].rearrange("p (s t) -> p s t", s=4),
                                       ACT.Copy).then_inc(S2["pTa_r"][c], 1)
                    act.wait_ge(S["WT_r"], b1)
                    act.activation(WTs[0:r, :, 0:r], bank[4][0:r, :].rearrange("p (s t) -> p s t", s=4)[:, :, 0:r],
                                   ACT.Copy).then_inc(S["WTs_r"], 1)
                    cc = cols(i, r)
                    act.wait_ge(S["mA_r"], b1)
                    act.activation(actH[:, 0:2, cc], mixA[:, :, 0:r], ACT.Copy).then_inc(S["hA_r"], 1)
                    if nx is not None:
                        front_late(nx)
                    act.wait_ge(S["pv_r"], b1)
                    act.activation(actH[:, 2:6, cc], bank[7][:, :].rearrange("p (s t) -> p s t", s=4)[:, :, 0:r],
                                   ACT.Copy).then_inc(S["hB_r"], 1)
                    act.wait_ge(S["hT_r"], b1)
                    act.activation(actH[:, 6:8, cc], bank[5][:, 0:2 * P].rearrange("p (s t) -> p s t", s=2)[:, :, 0:r],
                                   ACT.Copy).then_inc(S["hC_r"], 1)

                def mixer(b, nx):
                    if b is None:
                        front_early(nx)
                        front_late(nx)
                    else:
                        back(b, nx)

                each_block(mixer, act)
                act.wait_ge(stt_r, l + 1)
                act.activation(stout[:, 0:2], bank[0][0:HD + 1, 0:2 * P].rearrange("p (s k) -> p s k", s=2), ACT.Copy)
                act.activation(stout[:, 2:4], bank[1][0:HD + 1, 0:2 * P].rearrange("p (s k) -> p s k", s=2),
                               ACT.Copy).then_inc(sto_r, 1)

                M0 = l * (3 * N_USE)

                def split_w(s, slot, rslot, count, done):
                    act.wait_ge(raw_in[rslot], l * RAW_PER[rslot] + count)
                    if done is not None:
                        act.wait_ge(mm, M0 + done)
                    act.activation(wH[:, slot], raw[:, rslot], ACT.Copy).then_inc(w_h, 1)

                for s in range(6):
                    split_w(s, s, s % 3, RAW_AT[s], None)
                for m in range(KT):
                    split_w(m + 6, (m + 6) % 6, m % 3, RAW_AT[m + 6], 3 * (m + 1))
                    act.wait_ge(bank_free, M0 + 3 * (m + 1))
                    square(act, l * 2 + 1, m)
                for k in range(KT):
                    high_part(act, l * 2 + 1, k)

                def up_tile(q, f, slot):
                    act.wait_ge(up_r, l * (2 * NF) + q + 1)
                    if slot is None and not (isinstance(q, int) and q == 0):
                        act.wait_ge(g_l, l * NF + half(q))
                    if slot is not None:
                        act.wait_ge(gelu_r, l * NF + half(q - 1) + 1)
                    act.activation(cv[:, :], upb[:, PAD:], ACT.Identity, scale=convc[:, ds(f + 88, 1)],
                                   bias=convc[:, ds(f + 132, 1)]).then_inc(c0_r, 1)
                    if slot is None:
                        act.wait_ge(tap_r, l * (2 * NF) + q + 1)
                        act.activation(cu[:, :], cv[:, :], ACT.Gelu).then_inc(gelu_r, 1)
                    else:
                        act.wait_ge(gmul_r, l * NF + half(q - 1) + 1)
                        act.activation(gHL[:, slot, 0], cv[:, :], ACT.Copy).then_inc(g_h, 1)

                act.wait_ge(rstd_r, l * 5 + 5)
                for r, (f, slot) in enumerate(((0, None), (NF, 0), (1, None), (NF + 1, 2))):
                    up_tile(r, f, slot)
                    split_w(14 + r, 2 + r, (2 + r) % 3, RAW_AT[14 + r], 3 * (KT + r + 1))

                def group(n, par, ahead):
                    u = n * 12 + 12
                    up_tile(n * 4 + 4, n * 2 + 2, None)
                    split_ahead(n, 0, u * 3 + 3)
                    up_tile(n * 4 + 5, n * 2 + 2 + NF, 1 - par)
                    split_ahead(n, 1, u * 3 + 6)
                    if ahead:
                        split_ahead(n, 2, u * 3 + 30)
                        split_ahead(n, 3, u * 3 + 30)
                    up_tile(n * 4 + 6, n * 2 + 3, None)
                    if ahead:
                        split_ahead(n, 4, u * 3 + 33)
                    up_tile(n * 4 + 7, n * 2 + 3 + NF, 2)
                    if ahead:
                        split_ahead(n, 5, u * 3 + 36)

                def split_ahead(n, r, done):
                    split_w(n * 6 + 18 + r, r, r % 3, n * 32 + (RAW_12[r % 3] + 32 + 16 * (r // 3 + 1)), done)

                with act.Fori(0, (NG - 3) // 2) as j:
                    group(j * 2, 0, True)
                    group(j * 2 + 1, 1, True)
                group(NG - 3, 0, True)
                group(NG - 2, 1, False)
                for m in range(KT):
                    act.wait_ge(bank_free, M0 + 3 * (N_USE - KT + m + 1))
                    square(act, l * 2 + 2, m)
                    high_part(act, l * 2 + 2, m)
                act.wait_ge(cvt_r, l + 1)
                act.activation(cvo[:, :, :], bank[7][0:88, 0:256].rearrange("p (s t) -> p s t", s=2), ACT.Copy).then_inc(cvo_r, 1)

            act.wait_ge(x_done, DEPTH + 1)
            act.activation(identr[:, :], ident[:, :], ACT.Copy).then_inc(identr_r, 1)
            act.wait_ge(rt_r, 2 * DEPTH + 1)
            for i, (t0, r) in enumerate(TOK):
                act.wait_ge(y_tp, i + 1)
                wait(act, (y_st0, y_st1)[i % 2], 16 * (i // 2))
                act.activation(yst[0:r, i % 2, 0:512], bank[2 * (i % 2)][0:r, :], ACT.Copy, scale=rt[0:r, i:i + 1]).then_inc(y_ea, 1)

        @block.gpsimd
        def _(pool):
            pool.memset(ones[:, :], 1.0).then_inc(s_ones, 1)
            pool.memset(ms[:, :], 1.0).then_inc(s_ones, 1)
            pool.memset(mhalf[:, :], -0.5).then_inc(s_ones, 1)
            pool.wait_ge(s_ones, 3)
            norm_pool(pool, 0)
            with pool.Fori(0, DEPTH) as l:
                pool.wait_ge(par_in, (l + 1) * 336)
                settle(pool, settled)
                for t in (prob[0][:, :, :], prob[1][:, :, :], CN[0][:, :, :], qz[:, :, :], mp[0][:, :], vprev[0][:, :],
                          kTw[:, 0:P]):
                    pool.memset(t, 0.0).then_inc(init_r, 1)
                pool.memset(Vx[:, :, HD:HD + 1], 1.0).then_inc(init_r, 1)

                def mixer(b, nx):
                    if b is not None and b[4] in ("first", "mid"):
                        pool.wait_ge(S2["S_r"][1], l * 8 + b[1] + 1)
                        settle(pool, settled)
                        pool.tensor_copy(kTw[:, 0:P], kTw[:, P:2 * P]).then_inc(S["keepk_r"], 1)
                    if nx is not None:
                        par, i, zi, r, kind = nx
                        n1 = l * 9 + i + 1
                        z = zb[par]
                        pool.wait_ge(z_in[par], (l * Z_LOADS[par] + zi + 1) * 16)
                        qk = z[0:r, B_Q:B_Q + 640].rearrange("t (h d) -> t h d", h=10)
                        co = table[0:r, ds(i * ROT + CCOS, ROT)].rearrange("t (o d) -> t o d", o=1)
                        si = table[0:r, ds(i * ROT + CSIN, ROT)].rearrange("t (o d) -> t o d", o=1)
                        pool.tensor_tensor(rp1[0:r], qk[:, :, 0:ROT], co.broadcast_to([r, 10, ROT]), ALU.mult)
                        pool.tensor_tensor(rp2[0:r, :, 0:8], qk[:, :, 8:16], si[:, :, 0:8].broadcast_to([r, 10, 8]), ALU.mult)
                        pool.tensor_tensor(rp2[0:r, :, 8:16], qk[:, :, 0:8], si[:, :, 8:16].broadcast_to([r, 10, 8]),
                                           ALU.mult).then_inc(rp_r, 1)
                        pool.wait_ge(rp_r, n1)
                        pool.tensor_tensor(qk[:, :, 0:ROT], rp1[0:r], rp2[0:r], ALU.add).then_inc(S["rope_r"], 1)
                    if b is not None:
                        zc = zb[b[0]][0:b[3], C_K:C_K + 256].rearrange("p (h d) -> p h d", h=4)
                        pool.wait_ge(S["exk_r"], l * 9 + b[1] + 1)
                        pool.tensor_tensor(kw[0:b[3]].rearrange("p (h d) -> p h d", h=4), zc,
                                           exk[0:b[3]].rearrange("p (h o) -> p h o", o=1).broadcast_to([b[3], 4, HD]),
                                           ALU.mult).then_inc(S["kw_r"], 1)
                    if nx is not None:
                        pool.wait_ge(S["vms_r"], n1)
                        pool.tensor_tensor(rv[0:r], vss[0:r], mhalf[0:r, 0:1], ALU.pow).then_inc(S["rv_r"], 1)
                        pool.wait_ge(S["aa_r"], n1)
                        pool.tensor_tensor(dA[0:r, 0:4 * r].rearrange("p (h s) -> p h s", h=4),
                                           ident[0:r, 0:r].rearrange("p (o s) -> p o s", o=1).broadcast_to([r, 4, r]),
                                           aa[0:r].rearrange("p (h o) -> p h o", o=1).broadcast_to([r, 4, r]),
                                           ALU.mult).then_inc(S["dA_r"], 1)
                    if b is not None:
                        pool.wait_ge(S["kwmm_r"], l * 9 + b[1] + 1)
                        settle(pool, settled)
                        if b[4] in ("first", "mid"):
                            pool.tensor_copy(vprev[0][:, :], zb[b[0]][:, B_V:B_V + P]).then_inc(S["keepv_r"], 1)
                    if nx is not None:
                        pool.tensor_copy(Vx[0:r, :, 0:HD], z[0:r, C_V:C_V + 256].rearrange("t (h d) -> t h d", h=4)).then_inc(S["vx_r"], 1)

                each_block(mixer, pool)
                norm_pool(pool, l * 2 + 1)
                norm_pool(pool, l * 2 + 2)

        @block.vector
        def _(dve):
            def turn_x(par, t, c0, r):
                dve.wait_ge(xin_tp, t + 1)
                dve.tensor_copy(xT[:, 4:8, c0], bank[2 * par + 1][:, :].rearrange("p (k t) -> p k t", k=4)[:, :, 0:r]).then_inc(xin_ev, 1)

            dve.memset(xT[:, :, SEQ:SOFF], 0.0)
            turn_x(0, 0, ds(0, P), P)
            turn_x(1, 1, ds(P, P), P)
            with dve.Fori(1, 4) as j:
                turn_x(0, j * 2, ds(j * 256, P), P)
                turn_x(1, j * 2 + 1, ds(j * 256 + P, P), P)
            turn_x(0, 8, slice(SOFF, TC), DEC)
            dve.wait_ge(xin_ea, NTOK)
            dve.wait_ge(xin_ev, NTOK)
            dve.wait_ge(s_ones, 3)
            dve.memset(cu[:, 0:1], 0.0).then_inc(x_done, 1)
            dve.wait_ge(gains_r, 1)
            low_part(dve, 0, 0)
            for k in range(1, KT):
                add_square(dve, 0, k)
                low_part(dve, 0, k)
            mean_square(dve, 0)

            with dve.Fori(0, DEPTH) as l:
                def split_wz(g, par, w):
                    dve.wait_ge(wz_h, l * 5 + g + 1)
                    dve.tensor_tensor(wzL[par][:, :, 0:w], rawz[:, :, 0:w], wzH[par][:, :, 0:w].bitcast(F32),
                                      ALU.subtract).then_inc(wz_l, 1)

                split_wz(0, 0, ZA)
                for g in range(1, 5):
                    split_wz(g, g % 2, ZB)

                dve.wait_ge(par_in, (l + 1) * 336)
                dve.tensor_scalar(nsink[:, :], sink[:, :], -1.0, None, ALU.mult)
                dve.memset(gwT[64:128, :, 0:64], 0.0).then_inc(init_r, 1)
                dve.wait_ge(z_ev, l * 45 + 45)
                dve.memset(sm[:, :], 0.0).then_inc(init_r, 1)
                dve.wait_ge(init_r, l * INIT + INIT)

                def row(t, n, m):
                    return t.rearrange("p (h o) -> p h o", o=1).broadcast_to([t.shape[0], n, m])

                def flag(ins, s, n):
                    ins.then_inc(s, 1)
                    dve.wait_ge(s, n)

                def front_early(nx, link):
                    par, i, zi, r, kind = nx
                    n1 = l * 9 + i + 1
                    z = zb[par]
                    dve.wait_ge(z_in[par], (l * Z_LOADS[par] + zi + 1) * 16)
                    link(dve.tensor_tensor(g8[0:r], z[0:r, C_G:C_G + 8], gateb[0:r], ALU.add))
                    dve.scalar_tensor_tensor(ax[0:r], g8[0:r, 4:8], -1.0, g8[0:r, 4:8], ALU.mult, ALU.max).then_inc(S["ax_r"], 1)
                    dve.wait_ge(S["vss_r"], n1)
                    dve.tensor_scalar(vss[0:r], vss[0:r], 1.0 / 256, EPS, ALU.mult, ALU.add).then_inc(S["vms_r"], 1)

                def front_late(nx, link):
                    par, i, zi, r, kind = nx
                    n1 = l * 9 + i + 1
                    z = zb[par]
                    dve.wait_ge(S["lg_r"], n1)
                    dve.scalar_tensor_tensor(lf[0:r], g8[0:r, 4:8], 0.0, ax[0:r], ALU.min, ALU.subtract).then_inc(S["lf_r"], 1)
                    dve.wait_ge(S["tB_r"], n1)
                    dve.tensor_copy(bqT[:, :, 0:r], bank[1][:, :].rearrange("p (s t) -> p s t", s=4)[:, :, 0:r]).then_inc(S["bq_r"], 1)
                    dve.wait_ge(S["cum_r"], n1)
                    dve.tensor_copy(bb[0:r, 0:4], bank[3][0:r, 0:4])
                    flag(dve.tensor_copy(bb[:, 4:8], bank[3][:, 4:8]), S["bb_r"], n1)
                    flag(dve.tensor_tensor(aa[0:r], g8[0:r, 0:4], bb[0:r, 0:4], ALU.subtract), S["aa_r"], n1)
                    dve.wait_ge(S["rv_r"], n1)
                    dve.scalar_tensor_tensor(vn[0:r], z[0:r, A_V:A_V + 256], rv[0:r], ggain[0:r],
                                             ALU.mult, ALU.mult).then_inc(S["vn_r"], 1)

                def maxima(nx, link):
                    par, i, zi, r, kind = nx
                    for c in range(1 if kind == "sample" else 2):
                        k0, k1 = (128 if kind == "first" else 64 * c), 192 + 64 * c
                        dve.wait_ge(S2["S_r"][c], l * (9 - c) + i + 1)
                        for h in range(2):
                            t = dve.tensor_reduce(mx[:, c, 2 * h:2 * h + 2],
                                                  bank[2 * c + h][:, :].rearrange("p (s t) -> p s t", s=2)[:, :, k0:k1], AX.X, ALU.max)
                        link(t)
                        link(dve.scalar_tensor_tensor(nm[:, c], mx[:, c], -SCALE, nsink[:, :], ALU.mult, ALU.min))
                        dve.tensor_tensor(es[:, c], sink[:, :], nm[:, c], ALU.add).then_inc(S2["nm_r"][c], 1)

                def back(b, nx, link):
                    par, i, zi, r, kind = b
                    b1 = l * 9 + i + 1
                    c1 = l * 8 + i + 1
                    z = zb[par]
                    nch = 1 if kind == "sample" else 2
                    g = 1 if kind == "sample" else 0

                    def normalise(c):
                        k0, k1 = (128 if kind == "first" else 64 * c), 192 + 64 * c
                        dve.wait_ge(S2["e_r"][c], b1 if c == 0 else c1)
                        link(dve.tensor_tensor(rs[:, c], rs[:, c], es[:, c], ALU.add))
                        link(dve.reciprocal(rs[:, c], rs[:, c]))
                        for p in range(4):
                            t = dve.tensor_scalar(prob[c][:, p, k0:k1], prob[c][:, p, k0:k1], rs[:, c, p:p + 1], None, ALU.mult)
                        t.then_inc(S2["p_r"][c], 1)

                    normalise(0)
                    dve.wait_ge(S["A_r"], b1)
                    A = bank[6][:, 0:4 * r].rearrange("p (h s) -> p h s", h=4)
                    link(dve.tensor_tensor(Am[0:r, :, 0:r], A[0:r],
                                           table[0:r, CM:CM + r].rearrange("p (o s) -> p o s", o=1).broadcast_to([r, 4, r]), ALU.add))
                    dve.tensor_reduce(cm[0:r], Am[0:r, :, 0:r], AX.X, ALU.max)
                    flag(dve.tensor_reduce(G[:, :], A, AX.X, ALU.max), S["A_used"], b1)
                    dve.tensor_tensor(cm[0:r], cm[0:r], mp[g][0:r], ALU.max)
                    link(dve.tensor_tensor(G[:, :], G[:, :], mp[g][:, :], ALU.max))
                    dve.tensor_tensor(sm[0:r, 0:4], mp[g][0:r], cm[0:r], ALU.subtract)
                    dve.scalar_tensor_tensor(sm[0:r, 4:8], bb[0:r, 0:4], -1.0, cm[0:r], ALU.mult, ALU.subtract)
                    dve.tensor_tensor(sm[0:r, 8:12], aa[0:r], G[0:r], ALU.subtract)
                    flag(dve.tensor_tensor(sm[:, 12:16], mp[g][:, :], G[:, :], ALU.subtract), S["sm_r"], b1)
                    dve.tensor_tensor(mp[g][:, :], bb[:, 4:8], G[:, :], ALU.add)
                    dve.tensor_tensor(Am[0:r, :, 0:r], Am[0:r, :, 0:r], row(cm[0:r], 4, r), ALU.subtract).then_inc(S["D_r"], 1)
                    if nch == 2:
                        normalise(1)
                    dve.wait_ge(S["mix_r"], b1)
                    link(dve.tensor_tensor(mixA[:, :, 0:r], bank[7][:, 0:256].rearrange("p (s t) -> p s t", s=2)[:, :, 0:r],
                                           gbias[:, :, 0:r], ALU.add))
                    flag(dve.tensor_tensor(mixA[:, :, 0:r], mixA[:, :, 0:r], uT[:, :, 0:r], ALU.mult), S["mA_r"], b1)
                    dve.wait_ge(S["P_r"], b1)
                    dve.wait_ge(S["qk_r"], b1)
                    dve.tensor_tensor(Wt[0:r, :, 0:r], bank[4][0:r, :].rearrange("p (s t) -> p s t", s=4)[:, :, 0:r],
                                      Am[0:r, :, 0:r], ALU.mult).then_inc(S["W_r"], 1)
                    dve.wait_ge(S["ex_r"], b1)
                    dve.tensor_scalar(exk[0:r], ex[0:r, 8:12], SCALE, None, ALU.mult).then_inc(S["exk_r"], 1)
                    if nx is not None:
                        front_early(nx, link)
                    for c in range(nch):
                        dve.wait_ge(S2["PT_r"][c], b1 if c == 0 else c1)
                        dve.tensor_copy(pT[c][:, 0], bank[2 * c][:, :].rearrange("p (s t) -> p s t", s=4)).then_inc(S2["pTv_r"][c], 1)
                    dve.wait_ge(S["int_r"], b1)
                    link(dve.tensor_tensor(nd[0:r], bank[5][0:r, 0:260].rearrange("p (h d) -> p h d", h=4),
                                           row(ex[0:r, 0:4], 4, HD + 1), ALU.mult))
                    if nx is not None:
                        front_late(nx, link)
                    dve.wait_ge(S["num_r"], b1)
                    link(dve.tensor_tensor(nd[0:r], nd[0:r], bank[6][0:r, 0:260].rearrange("p (h d) -> p h d", h=4), ALU.add))
                    den = nd[0:r, :, HD:HD + 1].rearrange("p h o -> p (h o)")
                    link(dve.scalar_tensor_tensor(dn[0:r], den, -1.0, den, ALU.mult, ALU.max))
                    link(dve.tensor_tensor(dn[0:r], dn[0:r], ex[0:r, 4:8], ALU.max))
                    link(dve.reciprocal(dn[0:r], dn[0:r]))
                    h4 = hc[0:r].rearrange("p (h d) -> p h d", h=4)
                    link(dve.tensor_tensor(h4, nd[0:r, :, 0:HD], row(dn[0:r], 4, HD), ALU.mult))
                    dve.wait_ge(S["eo_r"], b1)
                    dve.tensor_tensor(hc[0:r], hc[0:r], eo[0:r], ALU.mult).then_inc(S["hc_r"], 1)
                    for h in range(2):
                        t = dve.tensor_copy(dec[64 * h:64 * h + 64, :],
                                            ex[64 * h:64 * h + 64, 12:16].rearrange("p (s h) -> p h s", h=2)[:, h])
                    link(t)
                    dve.wait_ge(S["kwmm_r"], b1)
                    if kind == "sample":
                        dve.wait_ge(cn_r, l * 2 + 2)
                    for s in range(2):
                        t = dve.scalar_tensor_tensor(CN[g][:, s], CN[g][:, s], dec[:, s:s + 1], bank[4][:, s * 65:s * 65 + 65],
                                                     ALU.mult, ALU.add)
                    t.then_inc(S["cn_up"], 1)
                    if nx is not None:
                        maxima(nx, link)
                    cc = cols(i, r)
                    dve.wait_ge(S["hA_r"], b1)
                    dve.tensor_tensor(actL[:, 0:2, cc], mixA[:, :, 0:r], actH[:, 0:2, cc].bitcast(F32), ALU.subtract)
                    dve.wait_ge(S["hB_r"], b1)
                    dve.tensor_tensor(actL[:, 2:6, cc], bank[7][:, :].rearrange("p (s t) -> p s t", s=4)[:, :, 0:r],
                                      actH[:, 2:6, cc].bitcast(F32), ALU.subtract)
                    dve.wait_ge(S["hC_r"], b1)
                    if kind in ("first", "mid"):
                        dve.wait_ge(S["keepv_r"], l * 7 + i + 1)
                    dve.tensor_tensor(actL[:, 6:8, cc], bank[5][:, 0:2 * P].rearrange("p (s t) -> p s t", s=2)[:, :, 0:r],
                                      actH[:, 6:8, cc].bitcast(F32), ALU.subtract).then_inc(S["blk_done"], 1)
                    dve.wait_ge(S["blk_done"], b1)
                    settle(dve, settled)

                def mixer(b, nx):
                    if b is None:
                        before, steps = 0, LINKS_FRONT
                    else:
                        before = LINKS_FRONT + b[1] * LINKS if b[4] != "sample" else LINKS_FRONT + 7 * LINKS + LINKS_LAST
                        steps = {"last": LINKS_LAST, "sample": LINKS_SAMPLE}.get(b[4], LINKS)
                    total = LINKS_FRONT + 7 * LINKS + LINKS_LAST + LINKS_SAMPLE
                    ch = Chain(dve, mix_seq, l * total + before)
                    if b is None:
                        front_early(nx, ch.link)
                        front_late(nx, ch.link)
                        maxima(nx, ch.link)
                    else:
                        back(b, nx, ch.link)
                    assert ch.n == steps, (b and b[4], ch.n)

                each_block(mixer, dve)
                dve.memset(actL[:, :, SEQ:SOFF].bitcast(F32), 0.0)
                dve.memset(actH[:, :, SEQ:SOFF].bitcast(F32), 0.0)

                M0 = l * (3 * N_USE)

                def split_w(s, slot, rslot):
                    dve.wait_ge(w_h, l * N_W + s + 1)
                    dve.tensor_tensor(wL[:, slot], raw[:, rslot], wH[:, slot].bitcast(F32), ALU.subtract).then_inc(w_l, 1)

                def add_x(u, m, uset):
                    for c, (t0, w) in enumerate(CH):
                        dve.wait_ge(mm, M0 + u * 3 + (c + 1))
                        t = dve.tensor_tensor(xT[:, m, t0:t0 + w], bank[3 * uset + c][:, 0:w], xT[:, m, t0:t0 + w], ALU.add)
                        t.then_inc(bank_free, 1)

                for s in range(6):
                    split_w(s, s, s % 3)
                for m in range(KT):
                    add_x(m, m, m % 2)
                    split_w(m + 6, (m + 6) % 6, m % 3)
                    if m:
                        add_square(dve, l * 2 + 1, m)
                mean_square(dve, l * 2 + 1)
                for k in range(KT):
                    low_part(dve, l * 2 + 1, k)
                dve.wait_ge(rt_r, l * 2 + 2)
                dve.tensor_tensor(diag[:, :, :], ident[:, :].rearrange("p (o s) -> p o s", o=1).broadcast_to([P, NTOK, P]),
                                  rt[:, :].rearrange("p (h o) -> p h o", o=1).broadcast_to([P, NTOK, P]), ALU.mult).then_inc(diag_r, 1)
                dve.wait_ge(rs_mm, l + 1)
                for s in range(2):
                    dve.tensor_copy(rstd[:, 384 * s:384 * s + 384], bank[3 + s][:, 0:384]).then_inc(rstd_r, 1)
                dve.tensor_copy(rstd[:, 768:1024], bank[5][:, 0:256]).then_inc(rstd_r, 1)
                dve.tensor_copy(rstd[:, SOFF:TC], bank[5][:, 256:320]).then_inc(rstd_r, 1)
                dve.memset(rstd[:, SEQ:SOFF], 0.0).then_inc(rstd_r, 1)
                dve.wait_ge(rstd_r, l * 5 + 5)
                dve.memset(upb[:, 0:PAD], 0.0)

                def up_tile(q, f, u, uset, slot, adds=None):
                    if slot is not None:
                        dve.wait_ge(tap_r, l * (2 * NF) + q)
                    for c, (t0, w) in enumerate(CH):
                        dve.wait_ge(mm, M0 + u * 3 + (c + 1))
                        dve.tensor_tensor(upb[:, PAD + t0:PAD + t0 + w], bank[3 * uset + c][:, 0:w], rstd[:, t0:t0 + w],
                                          ALU.mult).then_inc(bank_free, 1)
                    dve.wait_ge(bank_free, M0 + u * 3 + 3)
                    cache = convc[:, 176:264].rearrange("p (r a) -> p r a", r=2)
                    dve.tensor_copy(convst[:, 0:2, ds(f, 1)], upb[:, SEQ:SEQ + 2].rearrange("p (r o) -> p r o", o=1)).then_inc(cvs_r, 1)
                    dve.tensor_copy(convst[:, 2:4, ds(f, 1)], upb[:, TC:TC + 2].rearrange("p (r o) -> p r o", o=1)).then_inc(cvs_r, 1)
                    dve.tensor_copy(upb[:, SOFF:SOFF + 2].rearrange("p (r o) -> p r o", o=1), cache[:, :, ds(f, 1)]).then_inc(up_r, 1)
                    dve.wait_ge(c0_r, l * (2 * NF) + q + 1)
                    dve.scalar_tensor_tensor(cv[:, :], upb[:, 1:1 + TC], convc[:, ds(f + 44, 1)], cv[:, :], ALU.mult, ALU.add).then_inc(up_seq, 1)
                    if adds is not None:
                        add_x(adds, 0, 0)
                    dve.wait_ge(up_seq, l * (2 * NF) + q + 1)
                    dve.scalar_tensor_tensor(cv[:, :], upb[:, 0:TC], convc[:, ds(f, 1)], cv[:, :], ALU.mult, ALU.add).then_inc(tap_r, 1)
                    if adds is not None:
                        add_x(adds + 1, 1, 1)
                    if slot is not None:
                        dve.wait_ge(tap_r, l * (2 * NF) + q + 1)
                        dve.wait_ge(gelu_r, l * NF + half(q - 1) + 1)
                        dve.tensor_tensor(cv[:, :], cv[:, :], cu[:, :], ALU.mult).then_inc(gmul_r, 1)
                        if adds is not None:
                            add_x(adds + 2, 2, 0)
                        dve.wait_ge(g_h, l * NF + half(q - 1) + 1)
                        dve.tensor_tensor(gHL[:, slot, 1], cv[:, :], gHL[:, slot, 0].bitcast(F32), ALU.subtract).then_inc(g_l, 1)

                for r, (f, slot) in enumerate(((0, None), (NF, 0), (1, None), (NF + 1, 2))):
                    up_tile(r, f, KT + r, r % 2, slot)
                    split_w(14 + r, 2 + r, (2 + r) % 3)

                def group(n, par, ahead):
                    s, u = n * 6 + 18, n * 12 + 12
                    up_tile(n * 4 + 4, n * 2 + 2, u, 0, None)
                    split_w(s, 0, 0)
                    up_tile(n * 4 + 5, n * 2 + 2 + NF, u + 1, 1, 1 - par, u + 2)
                    split_w(s + 1, 1, 1)
                    for m in range(3, KT):
                        add_x(u + 2 + m, m, m % 2)
                    if ahead:
                        split_w(s + 2, 2, 2)
                        split_w(s + 3, 3, 0)
                    up_tile(n * 4 + 6, n * 2 + 3, u + 10, 0, None)
                    if ahead:
                        split_w(s + 4, 4, 1)
                    up_tile(n * 4 + 7, n * 2 + 3 + NF, u + 11, 1, 2)
                    if ahead:
                        split_w(s + 5, 5, 2)

                with dve.Fori(0, (NG - 3) // 2) as j:
                    group(j * 2, 0, True)
                    group(j * 2 + 1, 1, True)
                group(NG - 3, 0, True)
                group(NG - 2, 1, False)
                for m in range(KT):
                    add_x(N_USE - KT + m, m, m % 2)
                    if m:
                        if m > 1:
                            add_square(dve, l * 2 + 2, m - 1)
                        low_part(dve, l * 2 + 2, m - 1)
                add_square(dve, l * 2 + 2, KT - 1)
                low_part(dve, l * 2 + 2, KT - 1)
                mean_square(dve, l * 2 + 2)
                dve.wait_ge(bank_free, M0 + 3 * N_USE)
                dve.memset(convc[:, 0:1], 0.0).then_inc(x_done, 1)

            dve.wait_ge(rt_r, 2 * DEPTH + 1)
            for i, (t0, r) in enumerate(TOK):
                dve.wait_ge(y_tp, i + 1)
                wait(dve, (y_st0, y_st1)[i % 2], 16 * (i // 2))
                dve.tensor_scalar(yst[0:r, i % 2, 512:1024], bank[2 * (i % 2) + 1][0:r, :], rt[0:r, i:i + 1], None,
                                  ALU.mult).then_inc(y_ev, 1)


LINKS_FRONT, LINKS, LINKS_LAST, LINKS_SAMPLE = 5, 19, 17, 12
INIT = 10

RAW_AT, RAW_PER = {}, [0, 0, 0]
for _s in range(18):
    RAW_PER[_s % 3] += 64 if _s < KT else 16
    RAW_AT[_s] = RAW_PER[_s % 3]
RAW_12 = [RAW_AT[9], RAW_AT[10], RAW_AT[11]]
RAW_PER = [RAW_12[0] + 20 * 16 + 16, RAW_12[1] + 20 * 16 + 16, RAW_12[2] + 20 * 16]


def half(q):
    return q // 2 if isinstance(q, int) else q // 2


_INS = ["x_prompt", "x_sample", "cache_k", "cache_v", "state_C", "state_n", "state_m", "cache_conv", "attn_norm",
        "w_in", "gmlp_norm", "gmlp_w", "gmlp_b", "attn_sinks", "mlstm_gate_b", "w_out", "ffn_norm", "w_up",
        "conv_w", "conv_b", "w_down", "final_norm"]
_OUTS = [("y_prompt", (1, SEQ, D)), ("y_sample", (1, DEC, D)),
         ("prompt_k", (DEPTH, 1, P, 2, HD)), ("prompt_v", (DEPTH, 1, P, 2, HD)),
         ("prompt_C", (DEPTH, 1, 4, HD, HD)), ("prompt_n", (DEPTH, 1, 4, HD)), ("prompt_m", (DEPTH, 1, 4)),
         ("prompt_conv", (DEPTH, 1, 2, 2 * FF)),
         ("sample_gmlp_v", (DEPTH, 1, DEC, 256)), ("sample_k", (DEPTH, 1, DEC, 2, HD)), ("sample_v", (DEPTH, 1, DEC, 2, HD)),
         ("sample_C", (DEPTH, 1, 4, HD, HD)), ("sample_n", (DEPTH, 1, 4, HD)), ("sample_m", (DEPTH, 1, 4)),
         ("sample_conv", (DEPTH, 1, 2, 2 * FF))]


def kernel(**inputs):
    import concourse.bacc as bacc
    from concourse.bass_utils import run_bass_kernel_spmd

    nc = bacc.Bacc("TRN2", target_bir_lowering=False, num_devices=1)
    arrays = {f"in_{n}": np.ascontiguousarray(inputs[n]) for n in _INS}
    arrays["in_consts"] = constants()
    I = {n[3:]: nc.dram_tensor(n, a.shape, mybir.dt.from_np(a.dtype), kind="ExternalInput").ap() for n, a in arrays.items()}
    O = {n: nc.dram_tensor(f"out_{n}", s, F32, kind="ExternalOutput").ap() for n, s in _OUTS}
    build(nc, I, O)
    r = run_bass_kernel_spmd(nc, [arrays], core_ids=[0])
    return tuple(r.results[0][f"out_{n}"] for n, _ in _OUTS)
```
